# Optimizing a Trainium2 kernel written in Bass

```python
import jax, jax.numpy as jnp
from jax import lax
import numpy as np

D_MODEL = 1024
BATCH = 1
SEQ = 512
DEPTH = 1

MEM_LEN = 256
EPS = 1e-6

CHUNK = 128
A_GROUPS = 4
A_WIDTH = D_MODEL // 2
A_HEAD = A_WIDTH // A_GROUPS
B_WIDTH = D_MODEL // 2
CONV_WIDTH = 3
POOL_WINDOWS = (2, 4, 8, 16)
C_WIDTH = D_MODEL // 2
C_GROUP = C_WIDTH // len(POOL_WINDOWS)
N_BRANCH = 3
IN_SPLITS = (2 * A_WIDTH, 2 * A_WIDTH + 3 * B_WIDTH, 2 * A_WIDTH + 3 * B_WIDTH + C_WIDTH)
IN_COLS = 2 * A_WIDTH + 3 * B_WIDTH + C_WIDTH + N_BRANCH * D_MODEL
XATTN_HEADS = 4
XATTN_HEAD_DIM = D_MODEL // XATTN_HEADS
FFN_HIDDEN = ((-(-8 * D_MODEL // 3) + 255) // 256) * 256

kernel_name = "hybrid_gated_gmlp_conv_pool_xattn_block"

def rmsnorm(x, g):
    xf = x.astype(jnp.float32)
    y = xf * lax.rsqrt(jnp.mean(xf * xf, axis=-1, keepdims=True) + EPS)
    return (y * g.astype(jnp.float32)).astype(x.dtype)

def layernorm(x, g, b):
    xf = x.astype(jnp.float32)
    mu = jnp.mean(xf, axis=-1, keepdims=True)
    var = jnp.mean(jnp.square(xf - mu), axis=-1, keepdims=True)
    y = (xf - mu) * lax.rsqrt(var + EPS)
    return (y * g.astype(jnp.float32) + b.astype(jnp.float32)).astype(x.dtype)

def chunked_spatial_gating(z, ln_g, ln_b, ws, bs):
    u, v = jnp.split(z, 2, axis=-1)
    v = layernorm(v, ln_g, ln_b)
    nb, s, _ = v.shape
    v = v.reshape(nb, s // CHUNK, CHUNK, A_GROUPS, A_HEAD)
    causal = jnp.tril(jnp.ones((CHUNK, CHUNK), dtype=bool))
    w = jnp.where(causal[None], ws, jnp.zeros_like(ws)).astype(v.dtype)
    mixed = jnp.einsum('gij,bcjgd->bcigd', w, v) + bs.T.astype(v.dtype)[None, None, :, :, None]
    return u * mixed.reshape(nb, s, A_WIDTH)

def short_gated_conv(z, w_conv):
    gb, gc, xin = jnp.split(z, 3, axis=-1)
    y = gc * xin
    k = w_conv[:, None, :].astype(y.dtype)
    y = lax.conv_general_dilated(y, k, window_strides=(1,), padding=[(CONV_WIDTH - 1, 0)],
                                 dimension_numbers=('NWC', 'WIO', 'NWC'),
                                 feature_group_count=B_WIDTH)
    return gb * y

def multiscale_pool(z, wg, scale):
    nb, s, _ = z.shape
    zf = z.astype(jnp.float32)
    cs = jnp.concatenate([jnp.zeros((nb, 1, C_WIDTH), jnp.float32), jnp.cumsum(zf, axis=1)], axis=1)
    pos = jnp.arange(s)
    outs = []
    for gi, win in enumerate(POOL_WINDOWS):
        sl = slice(gi * C_GROUP, (gi + 1) * C_GROUP)
        seg = cs[:, :, sl]
        hi = seg[:, 1:]
        lo = jnp.concatenate([jnp.zeros((nb, win - 1, C_GROUP), jnp.float32), seg[:, :s - win + 1]], axis=1)
        count = jnp.minimum(pos + 1, win).astype(jnp.float32)[None, :, None]
        outs.append((hi - lo) / count - zf[:, :, sl])
    p = jnp.stack(outs, axis=2)
    p = jnp.einsum('bsgc,gcd->bsgd', p, wg.astype(jnp.float32)).reshape(nb, s, C_WIDTH)
    return (p * scale.astype(jnp.float32)).astype(z.dtype)

def mixer_block(x, g_mix, w_in, b_gate, a_ln_g, a_ln_b, a_ws, a_bs, b_conv, c_wg, c_scale,
                w_branch_a, w_branch_b, w_branch_c, w_o):
    nb, s, _ = x.shape
    h = rmsnorm(x, g_mix)
    proj = h @ w_in
    za, zb, zc, zg = jnp.split(proj, IN_SPLITS, axis=-1)
    ya = chunked_spatial_gating(jax.nn.gelu(za, approximate=False), a_ln_g, a_ln_b, a_ws, a_bs) @ w_branch_a
    yb = short_gated_conv(zb, b_conv) @ w_branch_b
    yc = multiscale_pool(zc, c_wg, c_scale) @ w_branch_c
    gates = jax.nn.sigmoid(zg.reshape(nb, s, N_BRANCH, D_MODEL) + b_gate)
    merged = gates[:, :, 0] * ya + gates[:, :, 1] * yb + gates[:, :, 2] * yc
    return x + merged @ w_o

def cross_attention(x, mem, g_x, g_m, w_q, w_kv, w_o):
    nb, s, _ = x.shape
    hq = rmsnorm(x, g_x)
    m = rmsnorm(mem, g_m)
    q = (hq @ w_q).reshape(nb, s, XATTN_HEADS, XATTN_HEAD_DIM)
    k, v = jnp.split(m @ w_kv, 2, axis=-1)
    k = k.reshape(nb, MEM_LEN, XATTN_HEADS, XATTN_HEAD_DIM)
    v = v.reshape(nb, MEM_LEN, XATTN_HEADS, XATTN_HEAD_DIM)
    sc = jnp.einsum('bshd,bmhd->bhsm', q, k).astype(jnp.float32) * (XATTN_HEAD_DIM ** -0.5)
    p = jax.nn.softmax(sc, axis=-1).astype(v.dtype)
    o = jnp.einsum('bhsm,bmhd->bshd', p, v).reshape(nb, s, D_MODEL)
    return x + o @ w_o

def swiglu_ffn(x, g, w_in, w_out):
    h = rmsnorm(x, g)
    gate, up = jnp.split(h @ w_in, 2, axis=-1)
    return x + (jax.nn.silu(gate) * up) @ w_out

def setup_inputs(seed: int = 0) -> dict:
    key = jax.random.key(seed)
    ks = jax.random.split(key, 32)
    f32 = jnp.float32
    L, D = DEPTH, D_MODEL

    def nrm(k, shape, fan_in):
        return jax.random.normal(k, shape, f32) * (fan_in ** -0.5)

    def gain(k, shape):
        return 1.0 + 0.02 * jax.random.normal(k, shape, f32)

    def small(k, shape, s=0.02):
        return s * jax.random.normal(k, shape, f32)

    return {
        "x": jax.random.normal(ks[0], (BATCH, SEQ, D), f32),
        "mem": jax.random.normal(ks[1], (BATCH, MEM_LEN, D), f32),
        "g_mix": gain(ks[2], (L, D)),
        "w_in": nrm(ks[3], (L, D, IN_COLS), D),
        "b_gate": small(ks[4], (L, N_BRANCH, D), 0.01),
        "a_ln_g": gain(ks[5], (L, A_WIDTH)),
        "a_ln_b": small(ks[6], (L, A_WIDTH)),
        "a_ws": nrm(ks[7], (L, A_GROUPS, CHUNK, CHUNK), CHUNK),
        "a_bs": gain(ks[8], (L, A_GROUPS, CHUNK)),
        "b_conv": nrm(ks[9], (L, CONV_WIDTH, B_WIDTH), CONV_WIDTH),
        "c_wg": nrm(ks[10], (L, len(POOL_WINDOWS), C_GROUP, C_GROUP), C_GROUP),
        "c_scale": gain(ks[11], (L, C_WIDTH)),
        "w_branch_a": nrm(ks[12], (L, A_WIDTH, D), A_WIDTH),
        "w_branch_b": nrm(ks[13], (L, B_WIDTH, D), B_WIDTH),
        "w_branch_c": nrm(ks[14], (L, C_WIDTH, D), C_WIDTH),
        "w_o": nrm(ks[15], (L, D, D), D),
        "g_xattn": gain(ks[16], (L, D)),
        "g_mem": gain(ks[17], (L, D)),
        "w_xq": nrm(ks[18], (L, D, D), D),
        "w_xkv": nrm(ks[19], (L, D, 2 * D), D),
        "w_xo": nrm(ks[20], (L, D, D), D),
        "g_ffn": gain(ks[21], (L, D)),
        "w_ffn_in": nrm(ks[22], (L, D, 2 * FFN_HIDDEN), D),
        "w_ffn_out": nrm(ks[23], (L, FFN_HIDDEN, D), FFN_HIDDEN),
        "g_final": gain(ks[24], (D,)),
    }

def reference(x, mem, g_mix, w_in, b_gate, a_ln_g, a_ln_b, a_ws, a_bs, b_conv, c_wg, c_scale,
              w_branch_a, w_branch_b, w_branch_c, w_o, g_xattn, g_mem, w_xq, w_xkv, w_xo,
              g_ffn, w_ffn_in, w_ffn_out, g_final):
    for l in range(DEPTH):
        x = mixer_block(x, g_mix[l], w_in[l], b_gate[l], a_ln_g[l], a_ln_b[l], a_ws[l], a_bs[l],
                        b_conv[l], c_wg[l], c_scale[l], w_branch_a[l], w_branch_b[l], w_branch_c[l], w_o[l])
        x = cross_attention(x, mem, g_xattn[l], g_mem[l], w_xq[l], w_xkv[l], w_xo[l])
        x = swiglu_ffn(x, g_ffn[l], w_ffn_in[l], w_ffn_out[l])
    return rmsnorm(x, g_final)


_drawn_inputs = setup_inputs


def setup_inputs(seed=0):
    import zlib

    import numpy as np

    out = dict(_drawn_inputs(seed))
    spreads = {}
    factors = {'g_mix': 2.699,
     'b_gate': 8.0,
     'a_ln_g': 8.0,
     'a_ln_b': 22.815,
     'a_bs': 8.0,
     'c_scale': 6.999,
     'g_xattn': 8.0,
     'g_mem': 8.0,
     'g_ffn': 15.335,
     'g_final': 8.145}
    for name, (base, spread) in spreads.items():
        noise = np.random.default_rng([zlib.crc32(name.encode()), seed]).standard_normal(out[name].shape)
        drawn = base * np.exp(spread * noise) if base else spread * noise
        out[name] = __import__('jax').numpy.asarray(drawn.astype(out[name].dtype))
    for name, factor in factors.items():
        out[name] = (out[name] * factor).astype(out[name].dtype)
    return out
```

```python
from contextlib import ExitStack

import numpy as np

import concourse.bass as bass
from concourse import mybir

F32 = mybir.dt.float32
F32R = mybir.dt.float32r
ACT = mybir.ActivationFunctionType
ALU = mybir.AluOpType
AX_X = mybir.AxisListType.X

P = 128
D = 1024
S = 512
M = 256
CHUNK = 128
HEADS = 4
HD = D // HEADS
HID = 2816
BW = 512
KT = D // P
TT = S // P
MT = M // P
BT = BW // P
HT = HID // P
EPS = 1e-6
PANEL = 2048
SLOTS = 2
PAD = 16

K0 = 0
V0 = K0 + 4
SV0 = V0 + 4
SU0 = SV0 + 2
GC0 = SU0 + 2
XI0 = GC0 + 2
PC0 = XI0 + 2
GB0 = PC0 + 2
GA0 = GB0 + 2
WO0 = GA0 + 18
Q0 = WO0 + 4
XO0 = Q0 + 4
FI0 = XO0 + 4
FO0 = FI0 + HT
PANELS = FO0 + HT // 2

C_MEM, C_MIX, C_X, C_FFN = 0, 8, 16, 24
C_BG = 32
C_SC = C_BG + 24
C_CV = C_SC + 4
C_BS = C_CV + 12
C_INV = C_BS + 4
COLS = C_INV + 4 * PAD


def build(nc, weights, x_in, mem_in, cols_in, sgu_in, wg_in, ln_g_in, ln_b_in, gf_in, out):
    base = -(-nc.sbuf_base // 32) * 32

    def at(name, kib, shape, dt=F32):
        return nc.alloc_sbuf_tensor_at(name, [P] + shape, dt, offset=base + int(kib * 1024))

    raw = at("raw", 0, [SLOTS, PANEL])
    wh = at("wh", 16, [SLOTS, PANEL], F32R)
    wl = at("wl", 32, [SLOTS, PANEL], F32R)
    X = at("X", 48, [KT, S])
    hh = at("hh", 64, [KT, S], F32R)
    hl = at("hl", 80, [KT, S], F32R)
    kh = at("kh", 96, [KT, M], F32R)
    kl = at("kl", 104, [KT, M], F32R)
    vh = at("vh", 112, [MT, D], F32R)
    vl = at("vl", 120, [MT, D], F32R)
    acth = at("acth", 128, [3 * BT, S], F32R)
    actl = at("actl", 152, [3 * BT, S], F32R)
    merged = at("merged", 176, [KT, S])
    memr = at("memr", 176, [KT, M])
    sq = at("sq", 184, [PANEL])
    memh = at("memh", 128, [KT, M], F32R)
    meml = at("meml", 136, [KT, M], F32R)
    xs = at("xs", 184, [4, S])
    acc_m = at("acc_m", 192, [M])
    acc_x = at("acc_x", 194, [S])
    var_m = at("var_m", 196, [M])
    var_x = at("var_x", 198, [S])
    rstd_x = at("rstd_x", 200, [S])
    rstd_m = at("rstd_m", 202, [M])
    vg = at("vg", 192, [TT, BW])
    svh = at("svh", 176, [TT, BW], F32R)
    svl = at("svl", 184, [TT, BW], F32R)
    ug = at("ug", 144, [TT, BW])
    ln_g = at("ln_g", 160, [BW])
    ln_b = at("ln_b", 162, [BW])
    wsr = at("wsr", 168, [4, CHUNK])
    wsh = at("wsh", 170, [4, CHUNK], F32R)
    wsl = at("wsl", 172, [4, CHUNK], F32R)
    cv = at("cv", 192, [BT, S])
    yp = at("yp", 200, [2, 4 + S])
    zp = at("zp", 176, [4, PAD + S])
    wgr = at("wgr", 184.5, [4, P])
    wgh = at("wgh", 186.5, [4, P], F32R)
    wgl = at("wgl", 188.5, [4, P], F32R)
    wa = at("wa", 200, [PAD + S])
    wb = at("wb", 202.0625, [PAD + S])
    sig = at("sig", 192, [4, S])
    mh = at("mh", 128, [KT, S], F32R)
    ml = at("ml", 152, [KT, S], F32R)
    oh = at("oh", 128, [KT, S], F32R)
    pth = at("pth", 144, [2, MT, S], F32R)
    ol = at("ol", 152, [KT, S], F32R)
    ptl = at("ptl", 168, [2, MT, S], F32R)
    qh = at("qh", 176, [2, 2, S], F32R)
    ql = at("ql", 184, [2, 2, S], F32R)
    pr = at("pr", 192, [2, TT, M])
    rstd_q = at("rstd_q", 200, [S])
    acc2 = at("acc2", 202, [S])
    sqt = at("sqt", 192, [S])
    hidh = at("hidh", 96, [HT, S], F32R)
    hidl = at("hidl", 140, [HT, S], F32R)
    gt = at("gt", 184, [2, S])
    ut = at("ut", 188, [2, S])
    gf = at("gf", 192, [D])
    rstd_f = at("rstd_f", 196, [S])
    outb = at("outb", 48, [TT, D])
    ones = at("ones", 204.25, [P])
    ident = at("ident", 204.75, [P])
    cols = at("cols", 205.25, [COLS])
    sm = at("sm", 205.875, [64])
    cst = at("cst", 206.25, [1])
    hd = at("hd", 206.5, [PAD])
    RM = 0
    VM = 4
    SU, SS, MU, VR, RS = 8, 12, 16, 20, 24
    MX, NB, SUM, REC = 28, 32, 36, 40
    FS, FV, FR = 44, 52, 56

    with ExitStack() as ctx:
        bank = [ctx.enter_context(nc.psum_tensor(f"bank{i}", [P, S], F32)) for i in range(8)]

        def sem(name):
            return ctx.enter_context(nc.semaphore(name))

        landed = [sem(f"landed{i}") for i in range(SLOTS)]
        hi_ready, lo_ready = sem("hi_ready"), sem("lo_ready")
        panel_done = sem("panel_done")
        mem_here, x_here, cols_here = sem("mem_here"), sem("x_here"), sem("cols_here")
        ln_here, ws_here, wg_here, gf_here = sem("ln_here"), sem("ws_here"), sem("wg_here"), sem("gf_here")
        const_ready = sem("const_ready")
        pool_step, dve_step, act_step = sem("pool_step"), sem("dve_step"), sem("act_step")
        memh_ready, meml_ready = sem("memh_ready"), sem("meml_ready")
        acc_m_ready, sums_m, var_m_ready, rstd_m_ready = sem("acc_m_ready"), sem("sums_m"), sem("var_m_ready"), sem("rstd_m_ready")
        acc_x_ready, sums_x, var_x_ready, rstd_x_ready = sem("acc_x_ready"), sem("sums_x"), sem("var_x_ready"), sem("rstd_x_ready")
        xs_ready, hh_ready, hl_ready = sem("xs_ready"), sem("hh_ready"), sem("hl_ready")
        k_even, k_scaled, kh_ready, kl_ready = sem("k_even"), sem("k_scaled"), sem("kh_ready"), sem("kl_ready")
        v_even, vh_ready, vl_ready = sem("v_even"), sem("vh_ready"), sem("vl_ready")
        sv_tile, sv_gelu, sv_centred, sv_squared, sv_var, sv_rstd, sv_normed, svh_ready, svl_ready = (
            sem(n) for n in ("sv_tile", "sv_gelu", "sv_centred", "sv_squared", "sv_var", "sv_rstd", "sv_normed", "svh_ready", "svl_ready"))
        su_tile, su_gelu = sem("su_tile"), sem("su_gelu")
        ws_masked, wsh_ready, wsl_ready = sem("ws_masked"), sem("wsh_ready"), sem("wsl_ready")
        mixed, a_tok, a_fm = sem("mixed"), sem("a_tok"), sem("a_fm")
        acth_ready, actl_ready = sem("acth_ready"), sem("actl_ready")
        gc_even, gc_ready, xi_even, pad_ready, cx_ready, pc_even, zp_ready = (
            sem(n) for n in ("gc_even", "gc_ready", "xi_even", "pad_ready", "cx_ready", "pc_even", "zp_ready"))
        gb_even, pooled, poolh_ready, pooll_ready, pool_lin, c_scaled, wgh_ready, wgl_ready = (
            sem(n) for n in ("gb_even", "pooled", "poolh_ready", "pooll_ready", "pool_lin", "c_scaled", "wgh_ready", "wgl_ready"))
        ga_even, br_tile, merged_ready, mh_ready, ml_ready = (
            sem(n) for n in ("ga_even", "br_tile", "merged_ready", "mh_ready", "ml_ready"))
        low_read = sem("low_read")
        high_read = sem("high_read")
        wo_even, x2_ready, acc_2, sums_2, var_2, rstd_2 = (
            sem(n) for n in ("wo_even", "x2_ready", "acc_2", "sums_2", "var_2", "rstd_2"))
        q_even, q_scaled, qh_ready, ql_ready = (sem(n) for n in ("q_even", "q_scaled", "qh_ready", "ql_ready"))
        scores, max_ready, exp_ready, probs, probs_t, pth_ready, ptl_ready, heads_out, oh_ready, ol_ready = (
            sem(n) for n in ("scores", "max_ready", "exp_ready", "probs", "probs_t", "pth_ready", "ptl_ready", "heads_out", "oh_ready", "ol_ready"))
        xo_even, x3_ready, acc_3, sums_3, var_3, rstd_3 = (
            sem(n) for n in ("xo_even", "x3_ready", "acc_3", "sums_3", "var_3", "rstd_3"))
        gate_even, up_even, g_scaled, u_scaled, silu_ready, u_prod, hidh_ready, hidl_ready = (
            sem(n) for n in ("gate_even", "up_even", "g_scaled", "u_scaled", "silu_ready", "u_prod", "hidh_ready", "hidl_ready"))
        fo_tile, f_sq, f_var, f_rstd, f_out, stored = (sem(n) for n in ("fo_tile", "f_sq", "f_var", "f_rstd", "f_out", "stored"))

        block = ctx.enter_context(nc.Block())

        def col(i):
            return cols[:, i:i + 1]

        def small(i, n=1):
            return sm[:, i:i + n]

        @block.sync
        def _(sp):
            sp.dma_start(memr[:], mem_in).then_inc(mem_here, 16)
            for n in range(SLOTS):
                sp.dma_start(raw[:, n, :], weights[n]).then_inc(landed[n], 16)
            sp.dma_start(X[:], x_in).then_inc(x_here, 16)
            with sp.Fori(1, PANELS // 2) as i:
                for s in range(SLOTS):
                    sp.wait_ge(lo_ready, 2 * i + (s - 1))
                    sp.dma_start(raw[:, s, :], weights[2 * i + s]).then_inc(landed[s], 16)
            sp.wait_ge(lo_ready, PANELS - 2)
            sp.dma_start(raw[:, 0, :], weights[PANELS - 1]).then_inc(landed[0], 16)
            for t in range(TT):
                sp.wait_ge(f_out, 2 * t + 2)
                sp.dma_start(out[t * P:(t + 1) * P, :], outb[:, t, :]).then_inc(stored, 16)
            sp.wait_ge(stored, 16 * TT)

        @block.gpsimd
        def _(pool):
            steps = [0]

            def chain(ins):
                steps[0] += 1
                ins.then_inc(pool_step, 1)
                pool.wait_ge(pool_step, steps[0])

            pool.dma_start(cols[:], cols_in).then_inc(cols_here, 16)
            pool.dma_start(ln_g[:], ln_g_in.to_broadcast([P, BW])).then_inc(ln_here, 16)
            pool.dma_start(ln_b[:], ln_b_in.to_broadcast([P, BW])).then_inc(ln_here, 16)
            pool.dma_start(wsr[:], sgu_in).then_inc(ws_here, 16)
            chain(nc.gpsimd.memset(ident[:], 0.0))
            nc.gpsimd.memset(ones[:], 1.0).then_inc(const_ready, 1)
            nc.gpsimd.memset(cst[:], -0.5).then_inc(const_ready, 1)
            nc.gpsimd.affine_select(out=ident[:], in_=ident[:], compare_op=ALU.not_equal, fill=1.0, base=0,
                                    pattern=[[-1, P]], channel_multiplier=1).then_inc(const_ready, 1)
            pool.wait_ge(const_ready, 3)

            def rsqrt(dst, src, n):
                return nc.gpsimd.tensor_tensor(dst, src, cst[:].to_broadcast([P, n]), ALU.pow)

            def fold(buf, n, last):
                while n > last:
                    n //= 2
                    chain(nc.gpsimd.tensor_tensor(buf[:, 0:n], buf[:, 0:n], buf[:, n:2 * n], ALU.add))

            pool.wait_ge(mem_here, 16)
            chain(nc.gpsimd.tensor_tensor(sq[:], memr[:].rearrange("p k m -> p (k m)"),
                                          memr[:].rearrange("p k m -> p (k m)"), ALU.mult))
            fold(sq, PANEL, 2 * M)
            chain(nc.gpsimd.tensor_tensor(acc_m[:], sq[:, 0:M], sq[:, M:2 * M], ALU.add))
            nc.gpsimd.tensor_copy(acc_m[:], acc_m[:]).then_inc(acc_m_ready, 1)
            pool.wait_ge(acc_m_ready, 1)
            pool.wait_ge(x_here, 16)
            for half in range(2):
                xv = X[:, 4 * half:4 * half + 4, :].rearrange("p k s -> p (k s)")
                chain(nc.gpsimd.tensor_tensor(sq[:], xv, xv, ALU.mult))
                fold(sq, PANEL, 2 * S)
                if half == 0:
                    chain(nc.gpsimd.tensor_tensor(acc_x[:], sq[:, 0:S], sq[:, S:2 * S], ALU.add))
                else:
                    chain(nc.gpsimd.tensor_tensor(sq[:, 0:S], sq[:, 0:S], sq[:, S:2 * S], ALU.add))
                    nc.gpsimd.tensor_tensor(acc_x[:], acc_x[:], sq[:, 0:S], ALU.add).then_inc(acc_x_ready, 1)
            pool.wait_ge(var_m_ready, 2)
            rsqrt(rstd_m[:], var_m[:], M).then_inc(rstd_m_ready, 1)
            rsqrt(small(RM, MT), small(VM, MT), MT).then_inc(rstd_m_ready, 1)
            pool.wait_ge(var_x_ready, 1)
            rsqrt(rstd_x[:], var_x[:], S).then_inc(rstd_x_ready, 1)
            pool.wait_ge(ws_here, 16)
            for g in range(4):
                nc.gpsimd.affine_select(out=wsr[:, g, :], in_=wsr[:, g, :], compare_op=ALU.is_ge, fill=0.0, base=0,
                                        pattern=[[1, CHUNK]], channel_multiplier=-1).then_inc(ws_masked, 1)
            for t in range(TT):
                pool.wait_ge(sv_var, t + 1)
                rsqrt(small(RS + t), small(VR + t), 1).then_inc(sv_rstd, 1)
            pool.wait_ge(mixed, 4)
            pool.dma_start(wgr[:], wg_in).then_inc(wg_here, 16)

            def sum_squares(ready, done):
                for k in range(KT):
                    pool.wait_ge(ready, k + 1)
                    dst = acc2 if k == 0 else sqt
                    ins = nc.gpsimd.tensor_tensor(dst[:], X[:, k, :], X[:, k, :], ALU.mult)
                    chain(ins)
                    if k:
                        ins = nc.gpsimd.tensor_tensor(acc2[:], acc2[:], sqt[:], ALU.add)
                        if k < KT - 1:
                            chain(ins)
                        else:
                            ins.then_inc(done, 1)

            sum_squares(x2_ready, acc_2)
            pool.wait_ge(var_2, 1)
            rsqrt(rstd_q[:], rstd_q[:], S).then_inc(rstd_2, 1)
            sum_squares(x3_ready, acc_3)
            pool.wait_ge(acc_3, 1)
            pool.dma_start(gf[:], gf_in.to_broadcast([P, D])).then_inc(gf_here, 16)
            pool.wait_ge(var_3, 1)
            rsqrt(rstd_f[:], rstd_f[:], S).then_inc(rstd_3, 1)
            for t in range(TT):
                pool.wait_ge(f_var, t + 1)
                rsqrt(small(FR + t), small(FV + t), 1).then_inc(f_rstd, 1)

        @block.scalar
        def _(act):
            copy = lambda o, i, **kw: nc.scalar.activation(o, i, ACT.Copy, **kw)

            def split_hi(n):
                act.wait_ge(landed[n % SLOTS], 16 * (n // SLOTS + 1))
                if n >= SLOTS:
                    act.wait_ge(panel_done, n - SLOTS + 1)
                copy(wh[:, n % SLOTS, :], raw[:, n % SLOTS, :]).then_inc(hi_ready, 1)

            act.wait_ge(mem_here, 16)
            act.wait_ge(cols_here, 16)
            for k in range(KT):
                copy(memh[:, k, :], memr[:, k, :], scale=col(C_MEM + k)).then_inc(memh_ready, 1)
            split_hi(0)
            for n in range(4):
                split_hi(K0 + n + 1)
                for t in range(2):
                    i = 2 * n + t
                    act.wait_ge(k_scaled, i + 1)
                    copy(kh[:, i, :], bank[2 * (n % 2) + t][:, 0:M]).then_inc(kh_ready, 1)
            act.wait_ge(rstd_m_ready, 2)
            for half in range(2):
                if half == 0:
                    split_hi(V0 + 1)
                    split_hi(V0 + 2)
                else:
                    split_hi(V0 + 4)
                for mt in range(MT):
                    b = (6 if half == 0 else 4) + mt
                    if mt == 0:
                        act.wait_ge(v_even, half + 1)
                    else:
                        act.wait_ge(panel_done, V0 + 2 * half + 2)
                    copy(vh[:, mt, half * S:(half + 1) * S], bank[b][:], scale=small(RM + mt)).then_inc(vh_ready, 1)
                if half == 0:
                    split_hi(V0 + 3)
                    for k in range(KT):
                        act.wait_ge(xs_ready, k + 1)
                        copy(hh[:, k, :], xs[:, k % 4, :], scale=col(C_MIX + k)).then_inc(hh_ready, 1)
            split_hi(SV0 + 1)
            split_hi(SV0 + 2)
            for t in range(TT):
                if t < TT - 1:
                    act.wait_ge(sv_tile, t + 1)
                else:
                    act.wait_ge(panel_done, SV0 + 2)
                nc.scalar.activation(vg[:, t, :], bank[t][:], ACT.Gelu, accum_out=small(SU + t)).then_inc(sv_gelu, 1)
            act.wait_ge(ws_masked, 4)
            copy(wsh[:], wsr[:]).then_inc(wsh_ready, 1)
            split_hi(SU0 + 1)
            for t in range(TT):
                act.wait_ge(sv_centred, t + 1)
                nc.scalar.activation(svh[:, t, :], vg[:, t, :], ACT.Square, accum_out=small(SS + t)).then_inc(sv_squared, 1)
            for t in range(TT):
                act.wait_ge(sv_normed, t + 1)
                copy(svh[:, t, :], vg[:, t, :]).then_inc(svh_ready, 1)
            split_hi(SU0 + 2)
            for t in range(TT):
                if t < TT - 1:
                    act.wait_ge(su_tile, t + 1)
                else:
                    act.wait_ge(panel_done, SU0 + 2)
                nc.scalar.activation(ug[:, t, :], bank[4 + t][:], ACT.Gelu).then_inc(su_gelu, 1)
            act.wait_ge(svl_ready, TT)
            for n in range(2):
                split_hi(GC0 + n + 1)
                for t in range(2):
                    act.wait_ge(gc_even if t == 0 else panel_done, n + 1 if t == 0 else GC0 + n + 1)
                    copy(cv[:, 2 * n + t, :], bank[2 * n + t][:]).then_inc(gc_ready, 1)
            split_hi(XI0 + 1)
            split_hi(XI0 + 2)
            for g in range(BT):
                act.wait_ge(a_fm, g + 1)
                copy(acth[:, g, :], bank[4 + g][:]).then_inc(acth_ready, 1)
            for n in range(2):
                split_hi(PC0 + n + 1)
                for t in range(2):
                    act.wait_ge(pc_even if t == 0 else panel_done, n + 1 if t == 0 else PC0 + n + 1)
                    if n == 0 and t == 0:
                        act.wait_ge(pad_ready, 2)
                    copy(zp[:, 2 * n + t, PAD:PAD + S], bank[2 * n + t][:]).then_inc(zp_ready, 1)
            def pool_hi(g):
                act.wait_ge(pooled, g + 1)
                copy(acth[:, 2 * BT + g, :], zp[:, g, PAD:PAD + S]).then_inc(poolh_ready, 1)

            for n in range(2):
                split_hi(GB0 + n + 1)
                if n == 0:
                    act.wait_ge(wg_here, 16)
                    copy(wgh[:], wgr[:]).then_inc(wgh_ready, 1)
                for g in ((0, 1, 2), (3,))[n]:
                    pool_hi(g)
                for t in range(2):
                    i = 2 * n + t
                    act.wait_ge(low_read, i + 1)
                    copy(acth[:, BT + i, :], cv[:, i, :]).then_inc(acth_ready, 1)
            split_hi(GA0 + 1)
            for g in range(4):
                act.wait_ge(c_scaled, g + 1)
                copy(acth[:, 2 * BT + g, :], bank[4 + g][:]).then_inc(acth_ready, 1)
            for b in range(3):
                for half in range(2):
                    n0 = GA0 + 6 * b + 3 * half
                    for j in range(2):
                        if (b, half, j) != (0, 0, 0):
                            split_hi(n0 + j + 1)
                        for t in range(2):
                            i = 4 * half + 2 * j + t
                            if t == 0:
                                act.wait_ge(ga_even, 4 * b + 2 * half + j + 1)
                            else:
                                act.wait_ge(panel_done, n0 + j + 1)
                            if (b, half) in ((0, 1), (1, 0)):
                                act.wait_ge(high_read, 4 + 8 * b + 4 * half - 4 + 2 * j + t + 1)
                            elif b:
                                act.wait_ge(merged_ready, 8 * (b - 1) + 4 * half - 4 + 2 * j + t + 1)
                            nc.scalar.activation(sig[:, 2 * j + t, :], bank[2 * j + t][:], ACT.Sigmoid,
                                                 bias=col(C_BG + 8 * b + i)).then_inc(low_read, 1)
                    split_hi(n0 + 3)
                    if b == 2:
                        for t in range(4):
                            act.wait_ge(merged_ready, 8 + 4 * half + t + 1)
                            copy(mh[:, 4 * half + t, :], merged[:, 4 * half + t, :]).then_inc(mh_ready, 1)

            for n in range(4):
                split_hi(WO0 + n + 1)
                for t in range(2):
                    i = 2 * n + t
                    act.wait_ge(x2_ready, i + 1)
                    copy(hh[:, i, :], X[:, i, :], scale=col(C_X + i)).then_inc(hh_ready, 1)

            def q_hi(h):
                if h >= 2:
                    act.wait_ge(scores, h - 1)
                for t in range(2):
                    act.wait_ge(q_scaled, 2 * h + t + 1)
                    copy(qh[:, h % 2, t, :], bank[2 * (h % 2) + t][:]).then_inc(qh_ready, 1)

            def exps(h):
                act.wait_ge(max_ready, h + 1)
                if h >= 2:
                    act.wait_ge(probs_t, 2 * (h - 2) + 2)
                for t in range(TT):
                    nc.scalar.activation(pr[:, h % 2, t, :], bank[4 + t // 2][:, (t % 2) * M:(t % 2 + 1) * M], ACT.Exp,
                                         bias=small(NB + t), scale=float(HD) ** -0.5,
                                         accum_out=small(SUM + t)).then_inc(exp_ready, 1)

            def pt_hi(h):
                for mt in range(MT):
                    act.wait_ge(probs_t, 2 * h + mt + 1)
                    if h >= 2:
                        act.wait_ge(heads_out, 2 * (h - 2) + 2)
                    copy(pth[:, h % 2, mt, :], bank[6 + mt][:]).then_inc(pth_ready, 1)

            def o_hi(h):
                for t in range(2):
                    act.wait_ge(heads_out, 2 * h + t + 1)
                    copy(oh[:, 2 * h + t, :], bank[6 + t][:]).then_inc(oh_ready, 1)

            split_hi(Q0 + 1)
            q_hi(0)
            split_hi(Q0 + 2)
            q_hi(1)
            exps(0)
            split_hi(Q0 + 3)
            q_hi(2)
            pt_hi(0)
            exps(1)
            o_hi(0)
            split_hi(Q0 + 4)
            q_hi(3)
            pt_hi(1)
            exps(2)
            o_hi(1)
            split_hi(XO0 + 1)
            pt_hi(2)
            exps(3)
            o_hi(2)
            pt_hi(3)
            o_hi(3)
            for n in range(4):
                if n:
                    split_hi(XO0 + n + 1)
                for t in range(2):
                    i = 2 * n + t
                    act.wait_ge(x3_ready, i + 1)
                    copy(hh[:, i, :], X[:, i, :], scale=col(C_FFN + i)).then_inc(hh_ready, 1)
            with act.Fori(0, HT // 2) as it:
                for s in range(2):
                    slot = (s + 1) % 2
                    act.wait_ge(landed[slot], it * 16 + 16 * ((FI0 + 1 + s) // 2 + 1))
                    act.wait_ge(panel_done, it * 2 + (FI0 + s))
                    copy(wh[:, slot, :], raw[:, slot, :]).then_inc(hi_ready, 1)
                    if s == 0:
                        for t in range(2):
                            act.wait_ge(g_scaled, it * 2 + (t + 1))
                            nc.scalar.activation(gt[:, t, :], gt[:, t, :], ACT.Silu).then_inc(silu_ready, 1)
                for t in range(2):
                    act.wait_ge(u_prod, it * 2 + (t + 1))
                    copy(hidh[:, it * 2 + t, :], ut[:, t, :]).then_inc(hidh_ready, 1)
            for n in range(FO0 + 1, PANELS):
                split_hi(n)
            dump = raw[:].rearrange("p s (q c) -> p (s q) c", c=S)
            for t in range(TT):
                if t < TT - 1:
                    act.wait_ge(fo_tile, t + 1)
                else:
                    act.wait_ge(panel_done, PANELS)
                for half in range(2):
                    nc.scalar.activation(dump[:, 2 * t + half, :], bank[(4 + 2 * t + half) % 8][:], ACT.Square,
                                         accum_out=small(FS + 2 * t + half)).then_inc(f_sq, 1)

        @block.vector
        def _(dve):
            V = nc.vector
            steps = [0]

            def chain(ins):
                steps[0] += 1
                ins.then_inc(dve_step, 1)
                dve.wait_ge(dve_step, steps[0])

            def f32(ap):
                return ap.bitcast(F32)

            def lo(dst, v, hi):
                return V.tensor_tensor(dst, v, f32(hi), ALU.subtract)

            def lo_scaled(dst, v, scale, hi):
                return V.scalar_tensor_tensor(out=dst, in0=v, scalar=scale, in1=f32(hi), op0=ALU.mult, op1=ALU.subtract)

            def split_lo(n):
                dve.wait_ge(hi_ready, n + 1)
                lo(wl[:, n % SLOTS, :], raw[:, n % SLOTS, :], wh[:, n % SLOTS, :]).then_inc(lo_ready, 1)

            dve.wait_ge(cols_here, 16)
            for k in range(KT):
                dve.wait_ge(memh_ready, k + 1)
                lo_scaled(meml[:, k, :], memr[:, k, :], col(C_MEM + k), memh[:, k, :]).then_inc(meml_ready, 1)
            split_lo(0)
            split_lo(1)
            dve.wait_ge(sums_m, 1)
            V.tensor_scalar(var_m[:], bank[4][:, 0:M], 1.0 / D, EPS, ALU.mult, ALU.add).then_inc(var_m_ready, 1)
            V.tensor_scalar(small(VM, MT), bank[4][:, M:M + MT], 1.0 / D, EPS, ALU.mult, ALU.add).then_inc(var_m_ready, 1)
            dve.wait_ge(rstd_m_ready, 1)
            for n in range(4):
                if n:
                    split_lo(K0 + n + 1)
                for t in range(2):
                    i, b = 2 * n + t, bank[2 * (n % 2) + t]
                    dve.wait_ge(k_even if t == 0 else panel_done, n + 1)
                    V.tensor_tensor(b[:, 0:M], b[:, 0:M], rstd_m[:], ALU.mult).then_inc(k_scaled, 1)
                for t in range(2):
                    i, b = 2 * n + t, 2 * (n % 2) + t
                    dve.wait_ge(kh_ready, i + 1)
                    lo(kl[:, i, :], bank[b][:, 0:M], kh[:, i, :]).then_inc(kl_ready, 1)
            for half in range(2):
                if half == 0:
                    split_lo(V0 + 1)
                    split_lo(V0 + 2)
                    dve.wait_ge(sums_x, 1)
                    V.tensor_scalar(var_x[:], bank[0][:], 1.0 / D, EPS, ALU.mult, ALU.add).then_inc(var_x_ready, 1)
                else:
                    split_lo(V0 + 4)
                for mt in range(MT):
                    b = (6 if half == 0 else 4) + mt
                    dve.wait_ge(vh_ready, 2 * half + mt + 1)
                    cs = slice(half * S, (half + 1) * S)
                    lo_scaled(vl[:, mt, cs], bank[b][:], small(RM + mt), vh[:, mt, cs]).then_inc(vl_ready, 1)
                if half == 0:
                    split_lo(V0 + 3)
                    dve.wait_ge(rstd_x_ready, 1)
                    for k in range(KT + 1):
                        if k < KT:
                            V.tensor_tensor(xs[:, k % 4, :], X[:, k, :], rstd_x[:], ALU.mult).then_inc(xs_ready, 1)
                        if k:
                            dve.wait_ge(hh_ready, k)
                            lo_scaled(hl[:, k - 1, :], xs[:, (k - 1) % 4, :], col(C_MIX + k - 1),
                                      hh[:, k - 1, :]).then_inc(hl_ready, 1)
            split_lo(SV0 + 1)
            split_lo(SV0 + 2)
            V.memset(yp[:, :, 0:4], 0.0).then_inc(pad_ready, 1)
            for t in range(TT):
                dve.wait_ge(sv_gelu, t + 1)
                chain(V.tensor_scalar(small(MU + t), small(SU + t), -1.0 / BW, None, ALU.mult))
                V.tensor_scalar(vg[:, t, :], vg[:, t, :], small(MU + t), None, ALU.add).then_inc(sv_centred, 1)
            dve.wait_ge(wsh_ready, 1)
            lo(wsl[:], wsr[:], wsh[:]).then_inc(wsl_ready, 1)
            split_lo(SU0 + 1)
            dve.wait_ge(ln_here, 32)
            for t in range(TT):
                dve.wait_ge(sv_squared, t + 1)
                V.tensor_scalar(small(VR + t), small(SS + t), 1.0 / BW, EPS, ALU.mult, ALU.add).then_inc(sv_var, 1)
            for t in range(TT):
                dve.wait_ge(sv_rstd, t + 1)
                dve.wait_ge(sv_centred, t + 1)
                chain(V.scalar_tensor_tensor(out=vg[:, t, :], in0=vg[:, t, :], scalar=small(RS + t), in1=ln_g[:],
                                             op0=ALU.mult, op1=ALU.mult))
                V.tensor_tensor(vg[:, t, :], vg[:, t, :], ln_b[:], ALU.add).then_inc(sv_normed, 1)
            for t in range(TT):
                dve.wait_ge(svh_ready, t + 1)
                lo(svl[:, t, :], vg[:, t, :], svh[:, t, :]).then_inc(svl_ready, 1)
            split_lo(SU0 + 2)
            split_lo(GC0 + 1)
            split_lo(GC0 + 2)
            for g in range(4):
                dve.wait_ge(mixed, g + 1)
                dve.wait_ge(su_gelu, TT)
                dst = ug[:, :, g * P:(g + 1) * P]
                V.scalar_tensor_tensor(out=dst, in0=bank[4 + g][:].rearrange("p (c d) -> p c d", c=TT),
                                       scalar=col(C_BS + g), in1=dst, op0=ALU.add, op1=ALU.mult).then_inc(a_tok, 1)
            V.memset(zp[:, :, 0:PAD], 0.0).then_inc(pad_ready, 1)
            for n in range(2):
                split_lo(XI0 + n + 1)
                for t in range(2):
                    i = 2 * n + t
                    y, c = yp[:, i % 2, :], cv[:, i, :]
                    dve.wait_ge(xi_even if t == 0 else panel_done, n + 1 if t == 0 else XI0 + n + 1)
                    dve.wait_ge(gc_ready, i + 1)
                    V.tensor_tensor(y[:, 4:4 + S], bank[2 * n + t][:], c, ALU.mult).then_inc(cx_ready, 1)
                    dve.wait_ge(cx_ready, i + 1)
                    chain(V.tensor_scalar(c, y[:, 2:2 + S], col(C_CV + i), None, ALU.mult))
                    chain(V.scalar_tensor_tensor(out=c, in0=y[:, 3:3 + S], scalar=col(C_CV + 4 + i), in1=c,
                                                 op0=ALU.mult, op1=ALU.add))
                    chain(V.scalar_tensor_tensor(out=c, in0=y[:, 4:4 + S], scalar=col(C_CV + 8 + i), in1=c,
                                                 op0=ALU.mult, op1=ALU.add))
            for g in range(BT):
                dve.wait_ge(acth_ready, g + 1)
                lo(actl[:, g, :], bank[4 + g][:], acth[:, g, :]).then_inc(actl_ready, 1)
            split_lo(PC0 + 1)
            split_lo(PC0 + 2)
            def pool_window(g):
                win = 2 << g
                src, length = zp[:, g, :], PAD + S
                z = zp[:, g, PAD:PAD + S]
                dve.wait_ge(zp_ready, g + 1)
                for lvl in range(g + 1):
                    sh, first = 1 << lvl, (2 << lvl) - 1
                    dst = (wa, wb)[lvl % 2]
                    chain(V.tensor_tensor(dst[:, first:length], src[:, first:length], src[:, first - sh:length - sh], ALU.add))
                    src = dst
                head = cols[:, C_INV + g * PAD:C_INV + (g + 1) * PAD]
                chain(V.tensor_tensor(hd[:], src[:, PAD:2 * PAD], head, ALU.mult))
                chain(V.tensor_tensor(hd[:], hd[:], z[:, 0:PAD], ALU.subtract))
                chain(V.scalar_tensor_tensor(out=z, in0=src[:, PAD:PAD + S], scalar=1.0 / win, in1=z,
                                             op0=ALU.mult, op1=ALU.subtract))
                V.tensor_copy(z[:, 0:PAD], hd[:]).then_inc(pooled, 1)

            def pool_lo(g):
                dve.wait_ge(poolh_ready, g + 1)
                lo(actl[:, 2 * BT + g, :], zp[:, g, PAD:PAD + S], acth[:, 2 * BT + g, :]).then_inc(pooll_ready, 1)

            for n in range(2):
                split_lo(GB0 + n + 1)
                if n == 0:
                    dve.wait_ge(wgh_ready, 1)
                    lo(wgl[:], wgr[:], wgh[:]).then_inc(wgl_ready, 1)
                    pool_window(0)
                    pool_window(1)
                    pool_lo(0)
                    pool_window(2)
                    pool_lo(1)
                else:
                    pool_window(3)
                    pool_lo(2)
                    pool_lo(3)
                for t in range(2):
                    i = 2 * n + t
                    dve.wait_ge(gb_even if t == 0 else panel_done, n + 1 if t == 0 else GB0 + n + 1)
                    V.tensor_tensor(cv[:, i, :], bank[2 * n + t][:], cv[:, i, :], ALU.mult).then_inc(low_read, 1)
                for t in range(2):
                    i = 2 * n + t
                    dve.wait_ge(acth_ready, BT + i + 1)
                    lo(actl[:, BT + i, :], cv[:, i, :], acth[:, BT + i, :]).then_inc(actl_ready, 1)
            split_lo(GA0 + 1)
            for g in range(4):
                dve.wait_ge(pool_lin, g + 1)
                V.tensor_scalar(bank[4 + g][:], bank[4 + g][:], col(C_SC + g), None, ALU.mult).then_inc(c_scaled, 1)
            for g in range(4):
                dve.wait_ge(acth_ready, 2 * BT + g + 1)
                lo(actl[:, 2 * BT + g, :], bank[4 + g][:], acth[:, 2 * BT + g, :]).then_inc(high_read, 1)
            def merged_lo(i):
                dve.wait_ge(mh_ready, i + 1)
                lo(ml[:, i, :], merged[:, i, :], mh[:, i, :]).then_inc(ml_ready, 1)

            for b in range(3):
                for half in range(2):
                    n0 = GA0 + 6 * b + 3 * half
                    for j in range(3):
                        if (b, half, j) != (0, 0, 0):
                            split_lo(n0 + j + 1)
                    for t in range(4):
                        i = 4 * half + t
                        seq = 8 * b + i
                        dve.wait_ge(low_read, 4 + seq + 1)
                        if t < 3:
                            dve.wait_ge(br_tile, 3 * (2 * b + half) + t + 1)
                        else:
                            dve.wait_ge(panel_done, n0 + 3)
                        dst = merged[:, i, :] if b == 0 else sig[:, t, :]
                        V.tensor_tensor(dst, bank[4 + t][:], sig[:, t, :], ALU.mult).then_inc(high_read, 1)
                        if b:
                            dve.wait_ge(high_read, 4 + seq + 1)
                            V.tensor_tensor(merged[:, i, :], merged[:, i, :], sig[:, t, :], ALU.add).then_inc(merged_ready, 1)
                        if b == 2 and t:
                            merged_lo(i - 1)
                    if b == 2:
                        merged_lo(4 * half + 3)

            def residual_lo(i, gain, first):
                dve.wait_ge(hh_ready, first + i + 1)
                lo_scaled(hl[:, i, :], X[:, i, :], col(gain + i), hh[:, i, :]).then_inc(hl_ready, 1)

            for n in range(4):
                split_lo(WO0 + n + 1)
                for t in range(2):
                    i = 2 * n + t
                    dve.wait_ge(wo_even if t == 0 else panel_done, n + 1 if t == 0 else WO0 + n + 1)
                    V.tensor_tensor(X[:, i, :], bank[2 * (n % 2) + t][:], X[:, i, :], ALU.add).then_inc(x2_ready, 1)
                    residual_lo(i, C_X, KT)

            def q_lo(h):
                for t in range(2):
                    b = 2 * (h % 2) + t
                    dve.wait_ge(q_even if t == 0 else panel_done, h + 1 if t == 0 else Q0 + h + 1)
                    V.tensor_tensor(bank[b][:], bank[b][:], rstd_q[:], ALU.mult).then_inc(q_scaled, 1)
                for t in range(2):
                    dve.wait_ge(qh_ready, 2 * h + t + 1)
                    lo(ql[:, h % 2, t, :], bank[2 * (h % 2) + t][:], qh[:, h % 2, t, :]).then_inc(ql_ready, 1)

            def softmax(h):
                dve.wait_ge(scores, h + 1)
                for b in range(2):
                    ins = V.tensor_reduce(small(MX + 2 * b, 2), bank[4 + b][:].rearrange("p (t m) -> p t m", t=2), AX_X, ALU.max)
                    chain(ins)
                V.tensor_scalar(small(NB, TT), small(MX, TT), -float(HD) ** -0.5, None, ALU.mult).then_inc(max_ready, 1)
                dve.wait_ge(exp_ready, TT * (h + 1))
                chain(V.reciprocal(small(REC, TT), small(SUM, TT)))
                for t in range(TT):
                    V.tensor_scalar(pr[:, h % 2, t, :], pr[:, h % 2, t, :], small(REC + t), None, ALU.mult).then_inc(probs, 1)

            def pt_lo(h):
                for mt in range(MT):
                    dve.wait_ge(pth_ready, 2 * h + mt + 1)
                    lo(ptl[:, h % 2, mt, :], bank[6 + mt][:], pth[:, h % 2, mt, :]).then_inc(ptl_ready, 1)

            def o_lo(h):
                for t in range(2):
                    dve.wait_ge(oh_ready, 2 * h + t + 1)
                    lo(ol[:, 2 * h + t, :], bank[6 + t][:], oh[:, 2 * h + t, :]).then_inc(ol_ready, 1)

            split_lo(Q0 + 1)
            dve.wait_ge(sums_2, 1)
            V.tensor_scalar(rstd_q[:], bank[4][:], 1.0 / D, EPS, ALU.mult, ALU.add).then_inc(var_2, 1)
            dve.wait_ge(rstd_2, 1)
            q_lo(0)
            split_lo(Q0 + 2)
            q_lo(1)
            softmax(0)
            split_lo(Q0 + 3)
            q_lo(2)
            pt_lo(0)
            softmax(1)
            o_lo(0)
            split_lo(Q0 + 4)
            q_lo(3)
            pt_lo(1)
            softmax(2)
            o_lo(1)
            split_lo(XO0 + 1)
            pt_lo(2)
            softmax(3)
            o_lo(2)
            pt_lo(3)
            o_lo(3)
            for n in range(4):
                if n:
                    split_lo(XO0 + n + 1)
                for t in range(2):
                    i = 2 * n + t
                    dve.wait_ge(xo_even if t == 0 else panel_done, n + 1 if t == 0 else XO0 + n + 1)
                    V.tensor_tensor(X[:, i, :], bank[2 * (n % 2) + t][:], X[:, i, :], ALU.add).then_inc(x3_ready, 1)
                    residual_lo(i, C_FFN, 2 * KT)
            dve.wait_ge(sums_3, 1)
            V.tensor_scalar(rstd_f[:], bank[4][:], 1.0 / D, EPS, ALU.mult, ALU.add).then_inc(var_3, 1)
            with dve.Fori(0, HT // 2) as it:
                for s in range(2):
                    slot = (s + 1) % 2
                    dve.wait_ge(hi_ready, it * 2 + (FI0 + 2 + s))
                    lo(wl[:, slot, :], raw[:, slot, :], wh[:, slot, :]).then_inc(lo_ready, 1)
                    if s == 0:
                        dve.wait_ge(rstd_3, 1)
                        for t in range(2):
                            dve.wait_ge(gate_even if t == 0 else panel_done, it * 1 + 1 if t == 0 else it * 2 + (FI0 + 1))
                            V.tensor_tensor(gt[:, t, :], bank[t][:], rstd_f[:], ALU.mult).then_inc(g_scaled, 1)
                for t in range(2):
                    dve.wait_ge(up_even if t == 0 else panel_done, it * 1 + 1 if t == 0 else it * 2 + (FI0 + 2))
                    V.tensor_tensor(ut[:, t, :], bank[2 + t][:], rstd_f[:], ALU.mult).then_inc(u_scaled, 1)
                    dve.wait_ge(u_scaled, it * 2 + (t + 1))
                    dve.wait_ge(silu_ready, it * 2 + (t + 1))
                    V.tensor_tensor(ut[:, t, :], ut[:, t, :], gt[:, t, :], ALU.mult).then_inc(u_prod, 1)
                    dve.wait_ge(hidh_ready, it * 2 + (t + 1))
                    lo(hidl[:, it * 2 + t, :], ut[:, t, :], hidh[:, it * 2 + t, :]).then_inc(hidl_ready, 1)
            for n in range(FO0 + 1, PANELS):
                split_lo(n)
            dve.wait_ge(gf_here, 16)
            for t in range(TT):
                dve.wait_ge(f_sq, 2 * t + 2)
                chain(V.tensor_tensor(small(FV + t), small(FS + 2 * t), small(FS + 2 * t + 1), ALU.add))
                V.tensor_scalar(small(FV + t), small(FV + t), 1.0 / D, EPS, ALU.mult, ALU.add).then_inc(f_var, 1)
                dve.wait_ge(f_rstd, t + 1)
                for half in range(2):
                    cs = slice(half * S, (half + 1) * S)
                    V.scalar_tensor_tensor(out=outb[:, t, cs], in0=bank[(4 + 2 * t + half) % 8][:], scalar=small(FR + t),
                                           in1=gf[:, cs], op0=ALU.mult, op1=ALU.mult).then_inc(f_out, 1)

        @block.tensor
        def _(pe):
            def mm3(dst, lh, ll, rh, rl, start, stop):
                nc.tensor.matmul(dst, lh, rh, start=start, stop=False)
                nc.tensor.matmul(dst, lh, rl, start=False, stop=False)
                return nc.tensor.matmul(dst, ll, rh, start=False, stop=stop)

            def fm_tile(dst, slot, t, rh, rl, ks=range(KT), first=0, ready=None, free=None):
                for k in ks:
                    if ready:
                        pe.wait_ge(ready[0], ready[1] + k + 1)
                    c = slice(k * 256 + t * P, k * 256 + (t + 1) * P)
                    ins = mm3(dst, wh[:, slot, c], wl[:, slot, c], rh(k), rl(k), k == 0, k == KT - 1)
                return ins

            def fm_panel(n, rh, rl, even, free, ready=None, width=S):
                pe.wait_ge(lo_ready, n + 1)
                for t in range(2):
                    if free:
                        pe.wait_ge(*free[t])
                    ins = fm_tile(bank[2 * (n % 2) + t][:, 0:width], n % SLOTS, t, rh, rl, ready=ready)
                    ins.then_inc(even if t == 0 else panel_done, 1)

            def tm_pair(n, banks, lhs, even, before=None):
                for half in range(2):
                    pe.wait_ge(lo_ready, n + half + 1)
                    for t, b in enumerate(banks):
                        if half == 0 and before:
                            before(t)
                        for k in range(4):
                            c = slice(k * S, (k + 1) * S)
                            slot = (n + half) % SLOTS
                            ins = mm3(bank[b][:], *lhs(4 * half + k, t), wh[:, slot, c], wl[:, slot, c],
                                      half == 0 and k == 0, half == 1 and k == 3)
                        if t == len(banks) - 1:
                            ins.then_inc(panel_done, 1)
                        elif half == 1:
                            ins.then_inc(even, 1)

            h_hi, h_lo = (lambda k: hh[:, k, :]), (lambda k: hl[:, k, :])

            for n in range(4):
                fm_panel(K0 + n, lambda k: memh[:, k, :], lambda k: meml[:, k, :], k_even,
                         [(kl_ready, 2 * (n - 2) + t + 1) for t in range(2)] if n >= 2 else None,
                         ready=(meml_ready, 0), width=M)
                if n == 0:
                    pe.wait_ge(acc_m_ready, 1)
                    pe.wait_ge(const_ready, 3)
                    nc.tensor.matmul(bank[4][:, 0:M], ones[:], acc_m[:], start=True, stop=True)
                    for mt in range(MT):
                        ins = nc.tensor.matmul(bank[4][:, M + mt:M + mt + 1], acc_m[:, mt * P:(mt + 1) * P], ones[:, 0:1],
                                               start=True, stop=True)
                    ins.then_inc(sums_m, 1)
            def mem_pair(k, t):
                return memh[:, k, t * P:(t + 1) * P], meml[:, k, t * P:(t + 1) * P]

            tm_pair(V0, (6, 7), mem_pair, v_even)
            pe.wait_ge(acc_x_ready, 1)
            pe.wait_ge(kl_ready, 2 * KT // 2)
            nc.tensor.matmul(bank[0][:], ones[:], acc_x[:], start=True, stop=True).then_inc(sums_x, 1)
            tm_pair(V0 + 2, (4, 5), mem_pair, v_even, before=lambda t: pe.wait_ge(var_m_ready, 2))

            def h_pair(k, t):
                return hh[:, k, t * P:(t + 1) * P], hl[:, k, t * P:(t + 1) * P]

            pe.wait_ge(hl_ready, KT)
            pe.wait_ge(var_x_ready, 1)
            tm_pair(SV0, (0, 1, 2, 3), h_pair, sv_tile)
            tm_pair(SU0, (4, 5, 6, 7), h_pair, su_tile, before=lambda t: pe.wait_ge(vl_ready, 4))
            for n in range(2):
                fm_panel(GC0 + n, h_hi, h_lo, gc_even, [(sv_gelu, 2 * n + t + 1) for t in range(2)])
            pe.wait_ge(svl_ready, TT)
            pe.wait_ge(wsl_ready, 1)
            for g in range(4):
                pe.wait_ge(su_gelu, g + 1)
                c = slice(g * P, (g + 1) * P)
                mm3(bank[4 + g][:].rearrange("p (c d) -> p c d", c=TT), wsh[:, g, :], wsl[:, g, :],
                    svh[:, :, c], svl[:, :, c], True, True).then_inc(mixed, 1)
            for n in range(2):
                fm_panel(XI0 + n, h_hi, h_lo, xi_even, [(gc_ready, 2 * n + t + 1) for t in range(2)])
            for g in range(4):
                pe.wait_ge(a_tok, g + 1)
                for t in range(TT):
                    ins = nc.tensor.transpose(bank[4 + g][:, t * P:(t + 1) * P], ug[:, t, g * P:(g + 1) * P], ident[:])
                ins.then_inc(a_fm, 1)
            for n in range(2):
                fm_panel(PC0 + n, h_hi, h_lo, pc_even, [(cx_ready, 2 * n + t + 1) for t in range(2)])
            for n in range(2):
                fm_panel(GB0 + n, h_hi, h_lo, gb_even, [(zp_ready, 2 * n + t + 1) for t in range(2)])
            pe.wait_ge(wgl_ready, 1)
            for g in range(4):
                pe.wait_ge(pooll_ready, g + 1)
                pe.wait_ge(actl_ready, g + 1)
                mm3(bank[4 + g][:], wgh[:, g, :], wgl[:, g, :], acth[:, 2 * BT + g, :], actl[:, 2 * BT + g, :],
                    True, True).then_inc(pool_lin, 1)

            def gate_panel(b, half, j):
                slot = (3 * half + j) % 2
                pe.wait_ge(lo_ready, b * 6 + (GA0 + 3 * half + j + 1))
                for t in range(2):
                    pe.wait_ge(low_read, b * 8 + (4 * half + 2 * j + t + 1))
                    ins = fm_tile(bank[2 * j + t][:], slot, t, h_hi, h_lo)
                    ins.then_inc(ga_even if t == 0 else panel_done, 1)

            def branch_panel(b, half):
                slot = (3 * half + 2) % 2
                pe.wait_ge(lo_ready, b * 6 + (GA0 + 3 * half + 3))
                for t in range(4):
                    pe.wait_ge(high_read, b * 8 + (4 * half + t + 1))
                    if t == 0:
                        pe.wait_ge(high_read, 4)
                        pe.wait_ge(actl_ready, 2 * BT)
                    for k in range(BT):
                        c = slice(k * S + t * P, k * S + (t + 1) * P)
                        ins = mm3(bank[4 + t][:], wh[:, slot, c], wl[:, slot, c], acth[:, b * BT + k, :],
                                  actl[:, b * BT + k, :], k == 0, k == BT - 1)
                    ins.then_inc(br_tile if t < 3 else panel_done, 1)

            with pe.Fori(0, 3) as b:
                for half in range(2):
                    gate_panel(b, half, 0)
                    gate_panel(b, half, 1)
                    branch_panel(b, half)
            for n in range(4):
                fm_panel(WO0 + n, lambda k: mh[:, k, :], lambda k: ml[:, k, :], wo_even,
                         [(low_read, 4 + 20 + 2 * n + t + 1) if n < 2 else (x2_ready, 2 * (n - 2) + t + 1) for t in range(2)],
                         ready=(ml_ready, 0))

            def q_panel(h):
                n = Q0 + h
                pe.wait_ge(lo_ready, n + 1)
                for t in range(2):
                    pe.wait_ge(*((x2_ready, 2 * (h + 2) + t + 1) if h < 2 else (ql_ready, 2 * (h - 2) + t + 1)))
                    ins = fm_tile(bank[2 * (h % 2) + t][:], n % SLOTS, t, h_hi, h_lo, ready=(hl_ready, KT))
                    ins.then_inc(q_even if t == 0 else panel_done, 1)
                    if h == 0 and t == 0:
                        pe.wait_ge(acc_2, 1)
                        pe.wait_ge(high_read, 4 + 20 + 1)
                        nc.tensor.matmul(bank[4][:], ones[:], acc2[:], start=True, stop=True).then_inc(sums_2, 1)

            def score(h):
                pe.wait_ge(ql_ready, 2 * h + 2)
                if h == 0:
                    pe.wait_ge(var_2, 1)
                    pe.wait_ge(high_read, 4 + 20 + 2)
                else:
                    pe.wait_ge(exp_ready, TT * h)
                for t in range(TT):
                    dst = bank[4 + t // 2][:, (t % 2) * M:(t % 2 + 1) * M]
                    for d in range(2):
                        c = slice(t * P, (t + 1) * P)
                        ins = mm3(dst, qh[:, h % 2, d, c], ql[:, h % 2, d, c], kh[:, 2 * h + d, :], kl[:, 2 * h + d, :],
                                  d == 0, d == 1)
                ins.then_inc(scores, 1)

            def transpose_probs(h):
                pe.wait_ge(probs, TT * (h + 1))
                if h == 0:
                    pe.wait_ge(high_read, 4 + 24)
                else:
                    pe.wait_ge(ol_ready, 2 * h)
                for mt in range(MT):
                    for t in range(TT):
                        ins = nc.tensor.transpose(bank[6 + mt][:, t * P:(t + 1) * P], pr[:, h % 2, t, mt * P:(mt + 1) * P], ident[:])
                    ins.then_inc(probs_t, 1)

            def head_out(h):
                pe.wait_ge(ptl_ready, 2 * h + 2)
                for t in range(2):
                    for mt in range(MT):
                        c = slice(h * HD + t * P, h * HD + (t + 1) * P)
                        ins = mm3(bank[6 + t][:], vh[:, mt, c], vl[:, mt, c], pth[:, h % 2, mt, :], ptl[:, h % 2, mt, :],
                                  mt == 0, mt == MT - 1)
                    ins.then_inc(heads_out, 1)

            def out_part(n, ks, done=False):
                pe.wait_ge(lo_ready, XO0 + n + 1)
                for t in range(2):
                    if ks[0] == 0:
                        pe.wait_ge(*((ql_ready, 2 * (n + 2) + t + 1) if n < 2 else (x3_ready, 2 * (n - 2) + t + 1)))
                    ins = fm_tile(bank[2 * (n % 2) + t][:], (XO0 + n) % SLOTS, t, lambda k: oh[:, k, :],
                                  lambda k: ol[:, k, :], ks=ks, ready=(ol_ready, 0))
                    if done:
                        ins.then_inc(xo_even if t == 0 else panel_done, 1)

            q_panel(0)
            q_panel(1)
            score(0)
            q_panel(2)
            transpose_probs(0)
            score(1)
            head_out(0)
            q_panel(3)
            transpose_probs(1)
            score(2)
            head_out(1)
            out_part(0, range(0, 4))
            transpose_probs(2)
            score(3)
            head_out(2)
            out_part(1, range(0, 4))
            transpose_probs(3)
            out_part(0, range(4, 6))
            out_part(1, range(4, 6))
            head_out(3)
            out_part(0, range(6, 8), True)
            out_part(1, range(6, 8), True)
            out_part(2, range(8), True)
            out_part(3, range(8), True)

            def ffn_in(it, first):
                for j in range(2):
                    n = FI0 + j
                    pe.wait_ge(lo_ready, it * 2 + (n + 1))
                    for t in range(2):
                        if first:
                            pe.wait_ge(x3_ready, 4 + 2 * j + t + 1)
                        else:
                            pe.wait_ge(g_scaled if j == 0 else u_scaled, it * 2 + (t - 1))
                        ins = fm_tile(bank[2 * j + t][:], n % SLOTS, t, h_hi, h_lo, ready=(hl_ready, 2 * KT) if first else None)
                        ins.then_inc((gate_even if j == 0 else up_even) if t == 0 else panel_done, 1)
                        if first and j == 0 and t == 0:
                            pe.wait_ge(acc_3, 1)
                            pe.wait_ge(exp_ready, TT * HEADS)
                            nc.tensor.matmul(bank[4][:], ones[:], acc2[:], start=True, stop=True).then_inc(sums_3, 1)

            ffn_in(0, True)
            with pe.Fori(1, HT // 2) as it:
                ffn_in(it, False)
            for n in range(HT // 2):
                pe.wait_ge(lo_ready, FO0 + n + 1)
                pe.wait_ge(hidl_ready, 2 * n + 2)
                slot = (FO0 + n) % SLOTS
                for t in range(TT):
                    for half in range(2):
                        b = (4 + 2 * t + half) % 8
                        if n == 0:
                            if b == 4:
                                pe.wait_ge(var_3, 1)
                                pe.wait_ge(ol_ready, 2 * HEADS)
                            elif b < 2:
                                pe.wait_ge(g_scaled, HT)
                            elif b < 4:
                                pe.wait_ge(u_scaled, HT)
                        if n == HT // 2 - 2:
                            for k in range(4):
                                nc.tensor.matmul(bank[b][:, k * P:(k + 1) * P], X[:, 4 * half + k, t * P:(t + 1) * P], ident[:],
                                                 start=False, stop=False, skip_group_check=True)
                        for k in range(2):
                            c = slice(k * D + half * S, k * D + (half + 1) * S)
                            r = slice(t * P, (t + 1) * P)
                            ins = mm3(bank[b][:], hidh[:, 2 * n + k, r], hidl[:, 2 * n + k, r], wh[:, slot, c], wl[:, slot, c],
                                      n == 0 and k == 0, n == HT // 2 - 1 and k == 1)
                    if t == TT - 1:
                        ins.then_inc(panel_done, 1)
                    elif n == HT // 2 - 1:
                        ins.then_inc(fo_tile, 1)


def fm(w):
    n = w.shape[1] // 256
    return w.reshape(KT, P, n, 256).transpose(2, 1, 0, 3).reshape(n, P, PANEL)


def tm(w, width):
    k = PANEL // width
    nk, nc_ = w.shape[0] // (k * P), w.shape[1] // width
    return w.reshape(nk, k, P, nc_, width).transpose(3, 0, 2, 1, 4).reshape(nk * nc_, P, PANEL)


def columns(v):
    return v.reshape(-1, P).T


def kernel(**inputs):
    import concourse.bacc as bacc
    from concourse.bass_utils import run_bass_kernel_spmd

    a = {k: np.asarray(v) for k, v in inputs.items()}
    w_in = a["w_in"][0]
    u, v, gb, gc, xi, pc, gates = np.split(w_in, [512, 1024, 1536, 2048, 2560, 3072], axis=1)
    gates = fm(gates)
    branch = [tm(a[n][0], 512) for n in ("w_branch_a", "w_branch_b", "w_branch_c")]
    ga = []
    for b in range(3):
        for half in range(2):
            ga += [gates[4 * b + 2 * half:4 * b + 2 * half + 2], branch[b][half:half + 1]]
    w_k, w_v = np.split(a["w_xkv"][0], 2, axis=1)
    f_gate, f_up = np.split(a["w_ffn_in"][0], 2, axis=1)
    ffn = np.stack([fm(f_gate), fm(f_up)], axis=1).reshape(HT, P, PANEL)
    weights = np.concatenate([fm(w_k), tm(w_v, 512), tm(v, 512), tm(u, 512), fm(gc), fm(xi), fm(pc), fm(gb)] + ga
                             + [fm(a["w_o"][0]), fm(a["w_xq"][0]), fm(a["w_xo"][0]), ffn, tm(a["w_ffn_out"][0], 1024)])
    inv = 1.0 / np.minimum(np.arange(PAD) + 1, np.array([[2], [4], [8], [16]])).astype(np.float32)
    cols = np.concatenate([columns(a[n][0]) for n in ("g_mem", "g_mix", "g_xattn", "g_ffn", "b_gate", "c_scale", "b_conv")]
                          + [a["a_bs"][0].T, np.broadcast_to(inv.astype(np.float32).reshape(1, -1), (P, 4 * PAD))], axis=1)
    arrays = {
        "weights": weights,
        "x": a["x"][0].T.reshape(KT, P, S).transpose(1, 0, 2),
        "mem": a["mem"][0].T.reshape(KT, P, M).transpose(1, 0, 2),
        "cols": cols,
        "sgu": a["a_ws"][0].transpose(2, 0, 1),
        "wg": a["c_wg"][0].transpose(1, 0, 2),
        "ln_g": a["a_ln_g"],
        "ln_b": a["a_ln_b"],
        "gf": a["g_final"].reshape(1, D),
    }
    arrays = {k: np.ascontiguousarray(v) for k, v in arrays.items()}
    nc = bacc.Bacc("TRN2", target_bir_lowering=False, num_devices=1)
    aps = [nc.dram_tensor(k, v.shape, mybir.dt.from_np(v.dtype), kind="ExternalInput").ap() for k, v in arrays.items()]
    out = nc.dram_tensor("out", (S, D), F32, kind="ExternalOutput").ap()
    build(nc, *aps, out)
    r = run_bass_kernel_spmd(nc, [arrays], core_ids=[0])
    return r.results[0]["out"].reshape(1, S, D)
```

```python
from contextlib import ExitStack

import numpy as np

from concourse import mybir

F32 = mybir.dt.float32
F32R = mybir.dt.float32r
ACT = mybir.ActivationFunctionType
ALU = mybir.AluOpType
AX_X = mybir.AxisListType.X

P = 128
D = 1024
S = 512
M = 256
CHUNK = 128
HEADS = 4
HD = D // HEADS
HID = 2816
BW = 512
KT = D // P
TT = S // P
MT = M // P
BT = BW // P
HT = HID // P
EPS = 1e-6
PANEL = 2048
SLOTS = 2
PAD = 16

K0 = 0
V0 = K0 + 4
SV0 = V0 + 4
SU0 = SV0 + 2
GC0 = SU0 + 2
XI0 = GC0 + 2
PC0 = XI0 + 2
GB0 = PC0 + 2
GA0 = GB0 + 2
WO0 = GA0 + 18
Q0 = WO0 + 4
XO0 = Q0 + 4
FI0 = XO0 + 4
FO0 = FI0 + HT
PANELS = FO0 + HT // 2

C_MEM, C_MIX, C_X, C_FFN = 0, 8, 16, 24
C_BG = 32
C_SC = C_BG + 24
C_CV = C_SC + 4
C_BS = C_CV + 12
C_INV = C_BS + 4
COLS = C_INV + 4 * PAD


def build(nc, weights, x_in, mem_in, cols_in, sgu_in, wg_in, ln_g_in, ln_b_in, gf_in, out):
    base = -(-nc.sbuf_base // 32) * 32

    def at(name, kib, shape, dt=F32):
        return nc.alloc_sbuf_tensor_at(name, [P] + shape, dt, offset=base + int(kib * 1024))

    raw = at("raw", 0, [SLOTS, PANEL])
    wh = at("wh", 16, [SLOTS, PANEL], F32R)
    wl = at("wl", 32, [SLOTS, PANEL], F32R)
    X = at("X", 48, [KT, S])
    hh = at("hh", 64, [KT, S], F32R)
    hl = at("hl", 80, [KT, S], F32R)
    kh = at("kh", 96, [KT, M], F32R)
    kl = at("kl", 104, [KT, M], F32R)
    vh = at("vh", 112, [MT, D], F32R)
    vl = at("vl", 120, [MT, D], F32R)
    acth = at("acth", 128, [3 * BT, S], F32R)
    actl = at("actl", 152, [3 * BT, S], F32R)
    merged = at("merged", 176, [KT, S])
    memr = at("memr", 176, [KT, M])
    sq = at("sq", 184, [PANEL])
    memh = at("memh", 128, [KT, M], F32R)
    meml = at("meml", 136, [KT, M], F32R)
    xs = at("xs", 184, [4, S])
    acc_m = at("acc_m", 192, [M])
    acc_x = at("acc_x", 194, [S])
    rstd_m = at("rstd_m", 200, [2 * M])
    vg = at("vg", 192, [TT, BW])
    svh = at("svh", 176, [TT, BW], F32R)
    svl = at("svl", 184, [TT, BW], F32R)
    ug = at("ug", 144, [TT, BW])
    ln_g = at("ln_g", 160, [BW])
    ln_b = at("ln_b", 162, [BW])
    wsr = at("wsr", 168, [4, CHUNK])
    wsh = at("wsh", 170, [4, CHUNK], F32R)
    wsl = at("wsl", 172, [4, CHUNK], F32R)
    cv = at("cv", 192, [BT, S])
    yp = at("yp", 200, [2, 4 + S])
    zp = at("zp", 176, [4, PAD + S])
    wgr = at("wgr", 184.5, [4, P])
    wgh = at("wgh", 186.5, [4, P], F32R)
    wgl = at("wgl", 188.5, [4, P], F32R)
    wa = at("wa", 200, [PAD + S])
    wb = at("wb", 202.0625, [PAD + S])
    sig = at("sig", 192, [4, S])
    mh = at("mh", 128, [KT, S], F32R)
    ml = at("ml", 152, [KT, S], F32R)
    oh = at("oh", 128, [KT, S], F32R)
    pth = at("pth", 144, [2, MT, S], F32R)
    ol = at("ol", 152, [KT, S], F32R)
    ptl = at("ptl", 168, [2, MT, S], F32R)
    qh = at("qh", 176, [2, 2, S], F32R)
    ql = at("ql", 184, [2, 2, S], F32R)
    pr = at("pr", 192, [2, TT, M])
    rstd_q = at("rstd_q", 200, [S])
    acc2 = at("acc2", 202, [S])
    sqt = at("sqt", 192, [S])
    hidh = at("hidh", 96, [HT, S], F32R)
    hidl = at("hidl", 140, [HT, S], F32R)
    gt = at("gt", 184, [2, S])
    ut = at("ut", 188, [2, S])
    gf = at("gf", 192, [D])
    rstd_f = at("rstd_f", 196, [S])
    outb = at("outb", 48, [TT, D])
    ones = at("ones", 204.25, [P])
    ident = at("ident", 204.75, [P])
    cols = at("cols", 205.25, [COLS])
    sm = at("sm", 205.875, [96])
    cst = at("cst", 206.25, [1])
    hd = at("hd", 206.5, [PAD])
    RM = 0
    VM = 4
    SU, SS, MU, VR, RS = 8, 12, 16, 20, 24
    MX, NB, SUM, REC = 28, 32, 36, 40
    FS, FV, FR = 44, 52, 56
    XV, XR, QV, QR, GV, GR = 60, 64, 68, 72, 76, 80

    with ExitStack() as ctx:
        bank = [ctx.enter_context(nc.psum_tensor(f"bank{i}", [P, S], F32)) for i in range(8)]

        def sem(name):
            return ctx.enter_context(nc.semaphore(name))

        landed = [sem(f"landed{i}") for i in range(SLOTS)]
        hi_ready, lo_ready = sem("hi_ready"), sem("lo_ready")
        panel_done = sem("panel_done")
        mem_here = [sem(f"mem_here{i}") for i in range(2)]
        x_here, cols_here = sem("x_here"), sem("cols_here")
        first_landed, half_hi, half_lo = sem("first_landed"), sem("half_hi"), sem("half_lo")
        ln_here, ws_here, wg_here, gf_here = sem("ln_here"), sem("ws_here"), sem("wg_here"), sem("gf_here")
        const_ready = sem("const_ready")
        pool_step, dve_step, table_loaded = sem("pool_step"), sem("dve_step"), sem("table_loaded")
        memh_ready, meml_ready = sem("memh_ready"), sem("meml_ready")
        acc_m_ready, sums_m, var_m_ready, rstd_m_ready, spread_m, spread_m_read = (
            sem(n) for n in ("acc_m_ready", "sums_m", "var_m_ready", "rstd_m_ready", "spread_m", "spread_m_read"))
        acc_x_ready, sums_x, var_x_ready, rstd_x_ready, spread_x = (
            sem(n) for n in ("acc_x_ready", "sums_x", "var_x_ready", "rstd_x_ready", "spread_x"))
        xs_ready, hh_ready, hl_ready = sem("xs_ready"), sem("hh_ready"), sem("hl_ready")
        k_scaled, kh_ready, kl_ready = sem("k_scaled"), sem("kh_ready"), sem("kl_ready")
        v_even, vh_ready, vl_ready = sem("v_even"), sem("vh_ready"), sem("vl_ready")
        sv_tile, sv_gelu, sv_centred, sv_squared, sv_var, sv_rstd, sv_normed, svh_ready, svl_ready = (
            sem(n) for n in ("sv_tile", "sv_gelu", "sv_centred", "sv_squared", "sv_var", "sv_rstd", "sv_normed", "svh_ready", "svl_ready"))
        su_tile, su_gelu = sem("su_tile"), sem("su_gelu")
        ws_masked, wsh_ready, wsl_ready = sem("ws_masked"), sem("wsh_ready"), sem("wsl_ready")
        mixed, a_tok, a_fm = sem("mixed"), sem("a_tok"), sem("a_fm")
        acth_ready, actl_ready = sem("acth_ready"), sem("actl_ready")
        gc_even, gc_ready, xi_even, pad_ready, cx_ready, pc_even, zp_ready = (
            sem(n) for n in ("gc_even", "gc_ready", "xi_even", "pad_ready", "cx_ready", "pc_even", "zp_ready"))
        gb_even, pooled, poolh_ready, pooll_ready, pool_lin, c_scaled, wgh_ready, wgl_ready = (
            sem(n) for n in ("gb_even", "pooled", "poolh_ready", "pooll_ready", "pool_lin", "c_scaled", "wgh_ready", "wgl_ready"))
        ga_even, br_tile, merged_ready, mh_ready, ml_ready = (
            sem(n) for n in ("ga_even", "br_tile", "merged_ready", "mh_ready", "ml_ready"))
        low_read = sem("low_read")
        high_read = sem("high_read")
        wo_even, x2_ready, acc_2, sums_2, var_2, rstd_2, spread_2, spread_2_read = (
            sem(n) for n in ("wo_even", "x2_ready", "acc_2", "sums_2", "var_2", "rstd_2", "spread_2", "spread_2_read"))
        q_even, q_scaled, qh_ready, ql_ready = (sem(n) for n in ("q_even", "q_scaled", "qh_ready", "ql_ready"))
        scores, max_ready, exp_ready, probs, probs_t, pth_ready, ptl_ready, heads_out, oh_ready, ol_ready = (
            sem(n) for n in ("scores", "max_ready", "exp_ready", "probs", "probs_t", "pth_ready", "ptl_ready", "heads_out", "oh_ready", "ol_ready"))
        xo_even, x3_ready, acc_3, sums_3, var_3, rstd_3, spread_3, spread_3_read = (
            sem(n) for n in ("xo_even", "x3_ready", "acc_3", "sums_3", "var_3", "rstd_3", "spread_3", "spread_3_read"))
        gate_even, up_even, g_scaled, u_scaled, silu_ready, u_prod, hidh_ready, hidl_ready = (
            sem(n) for n in ("gate_even", "up_even", "g_scaled", "u_scaled", "silu_ready", "u_prod", "hidh_ready", "hidl_ready"))
        fo_tile, f_sq, f_var, f_rstd, f_out, stored = (sem(n) for n in ("fo_tile", "f_sq", "f_var", "f_rstd", "f_out", "stored"))

        block = ctx.enter_context(nc.Block())

        def col(i):
            return cols[:, i:i + 1]

        def small(i, n=1):
            return sm[:, i:i + n]


        @block.sync
        def _(sp):
            half = PANEL // 2
            sp.dma_start(memr[:, 0:4, :], mem_in[:, 0:4, :]).then_inc(mem_here[0], 16)
            sp.dma_start(raw[:, 0, 0:half], weights[0, :, 0:half]).then_inc(first_landed, 16)
            sp.dma_start(memr[:, 4:8, :], mem_in[:, 4:8, :]).then_inc(mem_here[1], 16)
            sp.dma_start(raw[:, 0, half:PANEL], weights[0, :, half:PANEL]).then_inc(landed[0], 16)
            sp.dma_start(raw[:, 1, :], weights[1]).then_inc(landed[1], 16)
            sp.dma_start(X[:], x_in).then_inc(x_here, 16)
            with sp.Fori(1, PANELS // 2) as i:
                for s in range(SLOTS):
                    sp.wait_ge(lo_ready, 2 * i + (s - 1))
                    sp.dma_start(raw[:, s, :], weights[2 * i + s]).then_inc(landed[s], 16)
            sp.wait_ge(lo_ready, PANELS - 2)
            sp.dma_start(raw[:, 0, :], weights[PANELS - 1]).then_inc(landed[0], 16)
            for t in range(TT):
                for half in range(2):
                    sp.wait_ge(f_out, 2 * t + half + 1)
                    cs = slice(half * S, (half + 1) * S)
                    sp.dma_start(out[t * P:(t + 1) * P, cs], outb[:, t, cs]).then_inc(stored, 16)
            sp.wait_ge(stored, 16 * 2 * TT)

        @block.gpsimd
        def _(pool):
            steps = [0]

            def chain(ins):
                steps[0] += 1
                ins.then_inc(pool_step, 1)
                pool.wait_ge(pool_step, steps[0])

            nc.gpsimd.memset(cst[:], -0.5).then_inc(const_ready, 1)
            pool.dma_start(ln_g[:], ln_g_in.to_broadcast([P, BW])).then_inc(ln_here, 16)
            pool.dma_start(ln_b[:], ln_b_in.to_broadcast([P, BW])).then_inc(ln_here, 16)
            pool.dma_start(wsr[:], sgu_in).then_inc(ws_here, 16)
            chain(nc.gpsimd.memset(ident[:], 0.0))
            nc.gpsimd.memset(ones[:], 1.0).then_inc(const_ready, 1)
            nc.gpsimd.affine_select(out=ident[:], in_=ident[:], compare_op=ALU.not_equal, fill=1.0, base=0,
                                    pattern=[[-1, P]], channel_multiplier=1).then_inc(const_ready, 1)
            pool.wait_ge(const_ready, 3)

            def rsqrt(dst, src, n):
                return nc.gpsimd.tensor_tensor(dst, src, cst[:].to_broadcast([P, n]), ALU.pow)

            def fold(buf, n, last):
                while n > last:
                    n //= 2
                    chain(nc.gpsimd.tensor_tensor(buf[:, 0:n], buf[:, 0:n], buf[:, n:2 * n], ALU.add))

            for i in range(2):
                pool.wait_ge(mem_here[i], 16)
            chain(nc.gpsimd.tensor_tensor(sq[:], memr[:].rearrange("p k m -> p (k m)"),
                                          memr[:].rearrange("p k m -> p (k m)"), ALU.mult))
            fold(sq, PANEL, 2 * M)
            nc.gpsimd.tensor_tensor(acc_m[:], sq[:, 0:M], sq[:, M:2 * M], ALU.add).then_inc(acc_m_ready, 1)
            pool.wait_ge(acc_m_ready, 1)
            pool.wait_ge(var_m_ready, 1)
            rsqrt(small(RM, MT), small(VM, MT), MT).then_inc(rstd_m_ready, 1)
            pool.wait_ge(x_here, 16)
            for half in range(2):
                xv = X[:, 4 * half:4 * half + 4, :].rearrange("p k s -> p (k s)")
                chain(nc.gpsimd.tensor_tensor(sq[:], xv, xv, ALU.mult))
                fold(sq, PANEL, 2 * S)
                if half == 0:
                    chain(nc.gpsimd.tensor_tensor(acc_x[:], sq[:, 0:S], sq[:, S:2 * S], ALU.add))
                else:
                    chain(nc.gpsimd.tensor_tensor(sq[:, 0:S], sq[:, 0:S], sq[:, S:2 * S], ALU.add))
                    nc.gpsimd.tensor_tensor(acc_x[:], acc_x[:], sq[:, 0:S], ALU.add).then_inc(acc_x_ready, 1)
            pool.wait_ge(var_x_ready, 1)
            rsqrt(small(XR, TT), small(XV, TT), TT).then_inc(rstd_x_ready, 1)
            pool.wait_ge(ws_here, 16)
            for g in range(4):
                nc.gpsimd.affine_select(out=wsr[:, g, :], in_=wsr[:, g, :], compare_op=ALU.is_ge, fill=0.0, base=0,
                                        pattern=[[1, CHUNK]], channel_multiplier=-1).then_inc(ws_masked, 1)
            for t in range(TT):
                pool.wait_ge(sv_var, t + 1)
                rsqrt(small(RS + t), small(VR + t), 1).then_inc(sv_rstd, 1)
            pool.wait_ge(mixed, 4)
            pool.dma_start(wgr[:], wg_in).then_inc(wg_here, 16)

            def sum_squares(ready, done):
                for k in range(KT):
                    pool.wait_ge(ready, k + 1)
                    dst = acc2 if k == 0 else sqt
                    ins = nc.gpsimd.tensor_tensor(dst[:], X[:, k, :], X[:, k, :], ALU.mult)
                    chain(ins)
                    if k:
                        ins = nc.gpsimd.tensor_tensor(acc2[:], acc2[:], sqt[:], ALU.add)
                        if k < KT - 1:
                            chain(ins)
                        else:
                            ins.then_inc(done, 1)

            sum_squares(x2_ready, acc_2)
            pool.wait_ge(var_2, 1)
            rsqrt(small(QR, TT), small(QV, TT), TT).then_inc(rstd_2, 1)
            sum_squares(x3_ready, acc_3)
            pool.wait_ge(acc_3, 1)
            pool.dma_start(gf[:], gf_in.to_broadcast([P, D])).then_inc(gf_here, 16)
            pool.wait_ge(var_3, 1)
            rsqrt(small(GR, TT), small(GV, TT), TT).then_inc(rstd_3, 1)
            for t in range(TT):
                pool.wait_ge(f_var, t + 1)
                rsqrt(small(FR + t), small(FV + t), 1).then_inc(f_rstd, 1)

        @block.scalar
        def _(act):
            copy = lambda o, i, **kw: nc.scalar.activation(o, i, ACT.Copy, **kw)

            def split_hi(n):
                act.wait_ge(landed[n % SLOTS], 16 * (n // SLOTS + 1))
                if n >= SLOTS:
                    act.wait_ge(panel_done, n - SLOTS + 1)
                copy(wh[:, n % SLOTS, :], raw[:, n % SLOTS, :]).then_inc(hi_ready, 1)

            def split_hi_halves(n):
                act.wait_ge(landed[n % SLOTS], 16 * (n // SLOTS + 1))
                if n >= SLOTS:
                    act.wait_ge(panel_done, n - SLOTS + 1)
                for half in range(2):
                    cs = slice(half * PANEL // 2, (half + 1) * PANEL // 2)
                    copy(wh[:, n % SLOTS, cs], raw[:, n % SLOTS, cs]).then_inc(half_hi if half == 0 else hi_ready, 1)

            act.dma_start(cols[:], cols_in).then_inc(cols_here, 16)
            act.wait_ge(const_ready, 1)
            copy(hd[:, 0:1], cst[:]).then_inc(table_loaded, 1)
            act.wait_ge(cols_here, 16)
            for half in range(2):
                act.wait_ge(mem_here[half], 16)
                for k in range(4 * half, 4 * half + 4):
                    copy(memh[:, k, :], memr[:, k, :], scale=col(C_MEM + k)).then_inc(memh_ready, 1)
                act.wait_ge(first_landed if half == 0 else landed[0], 16)
                cs = slice(half * PANEL // 2, (half + 1) * PANEL // 2)
                copy(wh[:, 0, cs], raw[:, 0, cs]).then_inc(half_hi if half == 0 else hi_ready, 1)
            split_hi_halves(K0 + 1)
            split_hi_halves(K0 + 2)
            for n in range(4):
                if n == 1:
                    split_hi_halves(K0 + 3)
                elif n:
                    split_hi(K0 + n + 2)
                act.wait_ge(k_scaled, n + 1)
                copy(kh[:, 2 * n:2 * n + 2, :], bank[n][:].rearrange("p (t m) -> p t m", t=2)).then_inc(kh_ready, 1)
            act.wait_ge(rstd_m_ready, 1)
            for half in range(2):
                if half == 0:
                    split_hi(V0 + 2)
                for mt in range(MT):
                    b = (6 if half == 0 else 4) + mt
                    if mt == 0:
                        act.wait_ge(v_even, half + 1)
                    else:
                        act.wait_ge(panel_done, V0 + 2 * half + 2)
                    copy(vh[:, mt, half * S:(half + 1) * S], bank[b][:], scale=small(RM + mt)).then_inc(vh_ready, 1)
                if half == 0:
                    split_hi(V0 + 3)
                    for k in range(KT):
                        if k == 2:
                            split_hi(V0 + 4)
                        act.wait_ge(xs_ready, k + 1)
                        copy(hh[:, k, :], xs[:, k % 4, :], scale=col(C_MIX + k)).then_inc(hh_ready, 1)
            split_hi(SV0 + 1)
            split_hi(SV0 + 2)
            for t in range(TT):
                if t < TT - 1:
                    act.wait_ge(sv_tile, t + 1)
                else:
                    act.wait_ge(panel_done, SV0 + 2)
                nc.scalar.activation(vg[:, t, :], bank[t][:], ACT.Gelu, accum_out=small(SU + t)).then_inc(sv_gelu, 1)
            act.wait_ge(ws_masked, 4)
            copy(wsh[:], wsr[:]).then_inc(wsh_ready, 1)
            split_hi(SU0 + 1)
            for t in range(TT):
                act.wait_ge(sv_centred, t + 1)
                nc.scalar.activation(svh[:, t, :], vg[:, t, :], ACT.Square, accum_out=small(SS + t)).then_inc(sv_squared, 1)
            for t in range(TT):
                act.wait_ge(sv_normed, t + 1)
                copy(svh[:, t, :], vg[:, t, :]).then_inc(svh_ready, 1)
            split_hi(SU0 + 2)
            for t in range(TT):
                if t < TT - 1:
                    act.wait_ge(su_tile, t + 1)
                else:
                    act.wait_ge(panel_done, SU0 + 2)
                nc.scalar.activation(ug[:, t, :], bank[4 + t][:], ACT.Gelu).then_inc(su_gelu, 1)
            act.wait_ge(svl_ready, TT)
            for n in range(2):
                split_hi(GC0 + n + 1)
                for t in range(2):
                    act.wait_ge(gc_even if t == 0 else panel_done, n + 1 if t == 0 else GC0 + n + 1)
                    copy(cv[:, 2 * n + t, :], bank[2 * n + t][:]).then_inc(gc_ready, 1)
            split_hi(XI0 + 1)
            split_hi(XI0 + 2)
            for g in range(BT):
                act.wait_ge(a_fm, g + 1)
                copy(acth[:, g, :], bank[4 + g][:]).then_inc(acth_ready, 1)
            def pool_hi(g):
                act.wait_ge(pooled, g + 1)
                copy(acth[:, 2 * BT + g, :], zp[:, g, PAD:PAD + S]).then_inc(poolh_ready, 1)

            for n in range(2):
                split_hi(PC0 + n + 1)
                if n:
                    pool_hi(0)
                    pool_hi(1)
                for t in range(2):
                    act.wait_ge(pc_even if t == 0 else panel_done, n + 1 if t == 0 else PC0 + n + 1)
                    if n == 0 and t == 0:
                        act.wait_ge(pad_ready, 2)
                    copy(zp[:, 2 * n + t, PAD:PAD + S], bank[2 * n + t][:]).then_inc(zp_ready, 1)
            for n in range(2):
                split_hi(GB0 + n + 1)
                if n == 0:
                    act.wait_ge(wg_here, 16)
                    copy(wgh[:], wgr[:]).then_inc(wgh_ready, 1)
                pool_hi(2 + n)
                for t in range(2):
                    i = 2 * n + t
                    act.wait_ge(low_read, i + 1)
                    copy(acth[:, BT + i, :], cv[:, i, :]).then_inc(acth_ready, 1)
            split_hi(GA0 + 1)
            for g in range(4):
                act.wait_ge(c_scaled, g + 1)
                copy(acth[:, 2 * BT + g, :], bank[4 + g][:]).then_inc(acth_ready, 1)
            for b in range(3):
                for half in range(2):
                    n0 = GA0 + 6 * b + 3 * half
                    for j in range(2):
                        if (b, half, j) != (0, 0, 0):
                            split_hi(n0 + j + 1)
                        for t in range(2):
                            i = 4 * half + 2 * j + t
                            if t == 0:
                                act.wait_ge(ga_even, 4 * b + 2 * half + j + 1)
                            else:
                                act.wait_ge(panel_done, n0 + j + 1)
                            if (b, half) in ((0, 1), (1, 0)):
                                act.wait_ge(high_read, 4 + 8 * b + 4 * half - 4 + 2 * j + t + 1)
                            elif b:
                                act.wait_ge(merged_ready, 8 * (b - 1) + 4 * half - 4 + 2 * j + t + 1)
                            nc.scalar.activation(sig[:, 2 * j + t, :], bank[2 * j + t][:], ACT.Sigmoid,
                                                 bias=col(C_BG + 8 * b + i)).then_inc(low_read, 1)
                    split_hi(n0 + 3)
                    if b == 2:
                        for t in range(4):
                            act.wait_ge(merged_ready, 8 + 4 * half + t + 1)
                            copy(mh[:, 4 * half + t, :], merged[:, 4 * half + t, :]).then_inc(mh_ready, 1)

            for n in range(4):
                split_hi(WO0 + n + 1)
                for t in range(2):
                    i = 2 * n + t
                    act.wait_ge(x2_ready, i + 1)
                    copy(hh[:, i, :], X[:, i, :], scale=col(C_X + i)).then_inc(hh_ready, 1)

            def q_hi(h):
                if h >= 2:
                    act.wait_ge(scores, h - 1)
                for t in range(2):
                    act.wait_ge(q_scaled, 2 * h + t + 1)
                    copy(qh[:, h % 2, t, :], bank[2 * (h % 2) + t][:]).then_inc(qh_ready, 1)

            def exps(h):
                act.wait_ge(max_ready, h + 1)
                if h >= 2:
                    act.wait_ge(probs_t, 2 * (h - 2) + 2)
                for t in range(TT):
                    nc.scalar.activation(pr[:, h % 2, t, :], bank[4 + t // 2][:, (t % 2) * M:(t % 2 + 1) * M], ACT.Exp,
                                         bias=small(NB + t), scale=float(HD) ** -0.5,
                                         accum_out=small(SUM + t)).then_inc(exp_ready, 1)

            def pt_hi(h):
                for mt in range(MT):
                    act.wait_ge(probs_t, 2 * h + mt + 1)
                    if h >= 2:
                        act.wait_ge(heads_out, 2 * (h - 2) + 2)
                    copy(pth[:, h % 2, mt, :], bank[6 + mt][:]).then_inc(pth_ready, 1)

            def o_hi(h):
                for t in range(2):
                    act.wait_ge(heads_out, 2 * h + t + 1)
                    copy(oh[:, 2 * h + t, :], bank[6 + t][:]).then_inc(oh_ready, 1)

            split_hi(Q0 + 1)
            q_hi(0)
            split_hi(Q0 + 2)
            q_hi(1)
            exps(0)
            split_hi(Q0 + 3)
            q_hi(2)
            pt_hi(0)
            exps(1)
            o_hi(0)
            split_hi(Q0 + 4)
            q_hi(3)
            pt_hi(1)
            exps(2)
            o_hi(1)
            split_hi(XO0 + 1)
            pt_hi(2)
            exps(3)
            o_hi(2)
            pt_hi(3)
            o_hi(3)
            for n in range(4):
                if n > 1:
                    split_hi(XO0 + n + 1)
                for t in range(2):
                    i = 2 * n + t
                    if i == 1:
                        split_hi(XO0 + 2)
                    act.wait_ge(x3_ready, i + 1)
                    copy(hh[:, i, :], X[:, i, :], scale=col(C_FFN + i)).then_inc(hh_ready, 1)
            split_hi(FI0 + 1)
            with act.Fori(0, HT // 2) as it:
                for t in range(2):
                    act.wait_ge(g_scaled, it * 2 + (t + 1))
                    nc.scalar.activation(gt[:, t, :], gt[:, t, :], ACT.Silu).then_inc(silu_ready, 1)
                act.wait_ge(landed[0], it * 16 + 16 * ((FI0 + 2) // SLOTS + 1))
                act.wait_ge(panel_done, it * 2 + (FI0 + 1))
                copy(wh[:, 0, :], raw[:, 0, :]).then_inc(hi_ready, 1)
                for t in range(2):
                    act.wait_ge(u_prod, it * 2 + (t + 1))
                    copy(hidh[:, it * 2 + t, :], ut[:, t, :]).then_inc(hidh_ready, 1)
                act.wait_ge(landed[1], it * 16 + 16 * ((FI0 + 3) // SLOTS + 1))
                act.wait_ge(panel_done, it * 2 + (FI0 + 2))
                copy(wh[:, 1, :], raw[:, 1, :]).then_inc(hi_ready, 1)
            for n in range(FO0 + 2, PANELS):
                split_hi(n)
            dump = raw[:].rearrange("p s (q c) -> p (s q) c", c=S)
            for t in range(TT):
                for half in range(2):
                    if (t, half) == (TT - 1, 1):
                        act.wait_ge(panel_done, PANELS)
                    else:
                        act.wait_ge(fo_tile, 2 * t + half + 1)
                    nc.scalar.activation(dump[:, 2 * t + half, :], bank[(4 + 2 * t + half) % 8][:], ACT.Square,
                                         accum_out=small(FS + 2 * t + half)).then_inc(f_sq, 1)

        @block.vector
        def _(dve):
            V = nc.vector
            steps = [0]

            def chain(ins):
                steps[0] += 1
                ins.then_inc(dve_step, 1)
                dve.wait_ge(dve_step, steps[0])

            def f32(ap):
                return ap.bitcast(F32)

            def lo(dst, v, hi):
                return V.tensor_tensor(dst, v, f32(hi), ALU.subtract)

            def lo_scaled(dst, v, scale, hi):
                return V.scalar_tensor_tensor(out=dst, in0=v, scalar=scale, in1=f32(hi), op0=ALU.mult, op1=ALU.subtract)

            def split_lo(n):
                dve.wait_ge(hi_ready, n + 1)
                lo(wl[:, n % SLOTS, :], raw[:, n % SLOTS, :], wh[:, n % SLOTS, :]).then_inc(lo_ready, 1)

            def split_lo_halves(n):
                for half in range(2):
                    dve.wait_ge(half_hi if half == 0 else hi_ready, n + 1)
                    cs = slice(half * PANEL // 2, (half + 1) * PANEL // 2)
                    lo(wl[:, n % SLOTS, cs], raw[:, n % SLOTS, cs], wh[:, n % SLOTS, cs]).then_inc(
                        half_lo if half == 0 else lo_ready, 1)

            dve.wait_ge(cols_here, 16)
            for half in range(2):
                dve.wait_ge(mem_here[half], 16)
                for k in range(4 * half, 4 * half + 4):
                    dve.wait_ge(memh_ready, k + 1)
                    lo_scaled(meml[:, k, :], memr[:, k, :], col(C_MEM + k), memh[:, k, :]).then_inc(meml_ready, 1)
                dve.wait_ge(half_hi if half == 0 else hi_ready, 1)
                cs = slice(half * PANEL // 2, (half + 1) * PANEL // 2)
                lo(wl[:, 0, cs], raw[:, 0, cs], wh[:, 0, cs]).then_inc(half_lo if half == 0 else lo_ready, 1)
            split_lo_halves(K0 + 1)
            dve.wait_ge(sums_m, 1)
            V.tensor_scalar(small(VM, MT), bank[4][:, 0:MT], 1.0 / D, EPS, ALU.mult, ALU.add).then_inc(var_m_ready, 1)
            split_lo_halves(K0 + 2)
            dve.wait_ge(spread_m, 1)
            V.tensor_copy(rstd_m[:], bank[4][:]).then_inc(spread_m_read, 1)
            dve.wait_ge(spread_m_read, 1)
            for n in range(4):
                if n == 1:
                    split_lo_halves(K0 + 3)
                elif n:
                    split_lo(K0 + n + 2)
                dve.wait_ge(panel_done, K0 + n + 1)
                V.tensor_tensor(bank[n][:], bank[n][:], rstd_m[:], ALU.mult).then_inc(k_scaled, 1)
                dve.wait_ge(kh_ready, n + 1)
                lo(kl[:, 2 * n:2 * n + 2, :], bank[n][:].rearrange("p (t m) -> p t m", t=2),
                   kh[:, 2 * n:2 * n + 2, :]).then_inc(kl_ready, 1)
            for half in range(2):
                if half == 0:
                    dve.wait_ge(sums_x, 1)
                    V.tensor_scalar(small(XV, TT), bank[0][:, 0:TT], 1.0 / D, EPS, ALU.mult, ALU.add).then_inc(var_x_ready, 1)
                    split_lo(V0 + 2)
                for mt in range(MT):
                    b = (6 if half == 0 else 4) + mt
                    dve.wait_ge(vh_ready, 2 * half + mt + 1)
                    cs = slice(half * S, (half + 1) * S)
                    lo_scaled(vl[:, mt, cs], bank[b][:], small(RM + mt), vh[:, mt, cs]).then_inc(vl_ready, 1)
                if half == 0:
                    split_lo(V0 + 3)
                    dve.wait_ge(spread_x, 1)
                    for k in range(KT + 1):
                        if k < KT:
                            V.tensor_tensor(xs[:, k % 4, :], X[:, k, :], bank[3][:], ALU.mult).then_inc(xs_ready, 1)
                        if k == 2:
                            split_lo(V0 + 4)
                        if k:
                            dve.wait_ge(hh_ready, k)
                            lo_scaled(hl[:, k - 1, :], xs[:, (k - 1) % 4, :], col(C_MIX + k - 1),
                                      hh[:, k - 1, :]).then_inc(hl_ready, 1)
            split_lo(SV0 + 1)
            split_lo(SV0 + 2)
            V.memset(yp[:, :, 0:4], 0.0).then_inc(pad_ready, 1)
            for t in range(TT):
                dve.wait_ge(sv_gelu, t + 1)
                chain(V.tensor_scalar(small(MU + t), small(SU + t), -1.0 / BW, None, ALU.mult))
                V.tensor_scalar(vg[:, t, :], vg[:, t, :], small(MU + t), None, ALU.add).then_inc(sv_centred, 1)
            dve.wait_ge(wsh_ready, 1)
            lo(wsl[:], wsr[:], wsh[:]).then_inc(wsl_ready, 1)
            split_lo(SU0 + 1)
            dve.wait_ge(ln_here, 32)
            for t in range(TT):
                dve.wait_ge(sv_squared, t + 1)
                V.tensor_scalar(small(VR + t), small(SS + t), 1.0 / BW, EPS, ALU.mult, ALU.add).then_inc(sv_var, 1)
            for t in range(TT):
                dve.wait_ge(sv_rstd, t + 1)
                dve.wait_ge(sv_centred, t + 1)
                chain(V.scalar_tensor_tensor(out=vg[:, t, :], in0=vg[:, t, :], scalar=small(RS + t), in1=ln_g[:],
                                             op0=ALU.mult, op1=ALU.mult))
                V.tensor_tensor(vg[:, t, :], vg[:, t, :], ln_b[:], ALU.add).then_inc(sv_normed, 1)
            for t in range(TT):
                dve.wait_ge(svh_ready, t + 1)
                lo(svl[:, t, :], vg[:, t, :], svh[:, t, :]).then_inc(svl_ready, 1)
            split_lo(SU0 + 2)
            split_lo(GC0 + 1)
            split_lo(GC0 + 2)
            for g in range(4):
                dve.wait_ge(mixed, g + 1)
                dve.wait_ge(su_gelu, TT)
                dst = ug[:, :, g * P:(g + 1) * P]
                V.scalar_tensor_tensor(out=dst, in0=bank[4 + g][:].rearrange("p (c d) -> p c d", c=TT),
                                       scalar=col(C_BS + g), in1=dst, op0=ALU.add, op1=ALU.mult).then_inc(a_tok, 1)
            V.memset(zp[:, :, 0:PAD], 0.0).then_inc(pad_ready, 1)
            for n in range(2):
                split_lo(XI0 + n + 1)
                for t in range(2):
                    i = 2 * n + t
                    y, c = yp[:, i % 2, :], cv[:, i, :]
                    dve.wait_ge(xi_even if t == 0 else panel_done, n + 1 if t == 0 else XI0 + n + 1)
                    dve.wait_ge(gc_ready, i + 1)
                    V.tensor_tensor(y[:, 4:4 + S], bank[2 * n + t][:], c, ALU.mult).then_inc(cx_ready, 1)
                    dve.wait_ge(cx_ready, i + 1)
                    chain(V.tensor_scalar(c, y[:, 2:2 + S], col(C_CV + i), None, ALU.mult))
                    chain(V.scalar_tensor_tensor(out=c, in0=y[:, 3:3 + S], scalar=col(C_CV + 4 + i), in1=c,
                                                 op0=ALU.mult, op1=ALU.add))
                    chain(V.scalar_tensor_tensor(out=c, in0=y[:, 4:4 + S], scalar=col(C_CV + 8 + i), in1=c,
                                                 op0=ALU.mult, op1=ALU.add))
            for g in range(BT):
                dve.wait_ge(acth_ready, g + 1)
                lo(actl[:, g, :], bank[4 + g][:], acth[:, g, :]).then_inc(actl_ready, 1)
            def pool_window(g):
                win = 2 << g
                src, length = zp[:, g, :], PAD + S
                z = zp[:, g, PAD:PAD + S]
                dve.wait_ge(zp_ready, g + 1)
                for lvl in range(g + 1):
                    sh, first = 1 << lvl, (2 << lvl) - 1
                    dst = (wa, wb)[lvl % 2]
                    chain(V.tensor_tensor(dst[:, first:length], src[:, first:length], src[:, first - sh:length - sh], ALU.add))
                    src = dst
                head = cols[:, C_INV + g * PAD:C_INV + (g + 1) * PAD]
                chain(V.tensor_tensor(hd[:], src[:, PAD:2 * PAD], head, ALU.mult))
                chain(V.tensor_tensor(hd[:], hd[:], z[:, 0:PAD], ALU.subtract))
                chain(V.scalar_tensor_tensor(out=z, in0=src[:, PAD:PAD + S], scalar=1.0 / win, in1=z,
                                             op0=ALU.mult, op1=ALU.subtract))
                V.tensor_copy(z[:, 0:PAD], hd[:]).then_inc(pooled, 1)

            def pool_lo(g):
                dve.wait_ge(poolh_ready, g + 1)
                lo(actl[:, 2 * BT + g, :], zp[:, g, PAD:PAD + S], acth[:, 2 * BT + g, :]).then_inc(pooll_ready, 1)

            split_lo(PC0 + 1)
            split_lo(PC0 + 2)
            pool_window(0)
            pool_window(1)
            pool_lo(0)
            pool_lo(1)
            for n in range(2):
                split_lo(GB0 + n + 1)
                if n == 0:
                    dve.wait_ge(wgh_ready, 1)
                    lo(wgl[:], wgr[:], wgh[:]).then_inc(wgl_ready, 1)
                pool_window(2 + n)
                pool_lo(2 + n)
                for t in range(2):
                    i = 2 * n + t
                    dve.wait_ge(gb_even if t == 0 else panel_done, n + 1 if t == 0 else GB0 + n + 1)
                    V.tensor_tensor(cv[:, i, :], bank[2 * n + t][:], cv[:, i, :], ALU.mult).then_inc(low_read, 1)
                for t in range(2):
                    i = 2 * n + t
                    dve.wait_ge(acth_ready, BT + i + 1)
                    lo(actl[:, BT + i, :], cv[:, i, :], acth[:, BT + i, :]).then_inc(actl_ready, 1)
            split_lo(GA0 + 1)
            for g in range(4):
                dve.wait_ge(pool_lin, g + 1)
                V.tensor_scalar(bank[4 + g][:], bank[4 + g][:], col(C_SC + g), None, ALU.mult).then_inc(c_scaled, 1)
            for g in range(4):
                dve.wait_ge(acth_ready, 2 * BT + g + 1)
                lo(actl[:, 2 * BT + g, :], bank[4 + g][:], acth[:, 2 * BT + g, :]).then_inc(high_read, 1)
            def merged_lo(i):
                dve.wait_ge(mh_ready, i + 1)
                lo(ml[:, i, :], merged[:, i, :], mh[:, i, :]).then_inc(ml_ready, 1)

            for b in range(3):
                for half in range(2):
                    n0 = GA0 + 6 * b + 3 * half
                    for j in range(3):
                        if (b, half, j) != (0, 0, 0):
                            split_lo(n0 + j + 1)
                    for t in range(4):
                        i = 4 * half + t
                        seq = 8 * b + i
                        dve.wait_ge(low_read, 4 + seq + 1)
                        if t < 3:
                            dve.wait_ge(br_tile, 3 * (2 * b + half) + t + 1)
                        else:
                            dve.wait_ge(panel_done, n0 + 3)
                        dst = merged[:, i, :] if b == 0 else sig[:, t, :]
                        V.tensor_tensor(dst, bank[4 + t][:], sig[:, t, :], ALU.mult).then_inc(high_read, 1)
                        if b:
                            dve.wait_ge(high_read, 4 + seq + 1)
                            V.tensor_tensor(merged[:, i, :], merged[:, i, :], sig[:, t, :], ALU.add).then_inc(merged_ready, 1)
                        if b == 2 and t:
                            merged_lo(i - 1)
                    if b == 2:
                        merged_lo(4 * half + 3)

            def residual_lo(i, gain, first):
                dve.wait_ge(hh_ready, first + i + 1)
                lo_scaled(hl[:, i, :], X[:, i, :], col(gain + i), hh[:, i, :]).then_inc(hl_ready, 1)

            for n in range(4):
                split_lo(WO0 + n + 1)
                for t in range(2):
                    i = 2 * n + t
                    dve.wait_ge(wo_even if t == 0 else panel_done, n + 1 if t == 0 else WO0 + n + 1)
                    V.tensor_tensor(X[:, i, :], bank[2 * (n % 2) + t][:], X[:, i, :], ALU.add).then_inc(x2_ready, 1)
                    residual_lo(i, C_X, KT)

            def q_lo(h):
                for t in range(2):
                    b = 2 * (h % 2) + t
                    dve.wait_ge(q_even if t == 0 else panel_done, h + 1 if t == 0 else Q0 + h + 1)
                    V.tensor_tensor(bank[b][:], bank[b][:], rstd_q[:], ALU.mult).then_inc(q_scaled, 1)
                for t in range(2):
                    dve.wait_ge(qh_ready, 2 * h + t + 1)
                    lo(ql[:, h % 2, t, :], bank[2 * (h % 2) + t][:], qh[:, h % 2, t, :]).then_inc(ql_ready, 1)

            def softmax(h):
                dve.wait_ge(scores, h + 1)
                for b in range(2):
                    chain(V.tensor_reduce(small(MX + 2 * b, 2), bank[4 + b][:].rearrange("p (t m) -> p t m", t=2),
                                          AX_X, ALU.max))
                V.tensor_scalar(small(NB, TT), small(MX, TT), -float(HD) ** -0.5, None, ALU.mult).then_inc(max_ready, 1)
                dve.wait_ge(exp_ready, TT * (h + 1))
                chain(V.reciprocal(small(REC, TT), small(SUM, TT)))
                for t in range(TT):
                    V.tensor_scalar(pr[:, h % 2, t, :], pr[:, h % 2, t, :], small(REC + t), None, ALU.mult).then_inc(probs, 1)

            def pt_lo(h):
                for mt in range(MT):
                    dve.wait_ge(pth_ready, 2 * h + mt + 1)
                    lo(ptl[:, h % 2, mt, :], bank[6 + mt][:], pth[:, h % 2, mt, :]).then_inc(ptl_ready, 1)

            def o_lo(h):
                for t in range(2):
                    dve.wait_ge(oh_ready, 2 * h + t + 1)
                    lo(ol[:, 2 * h + t, :], bank[6 + t][:], oh[:, 2 * h + t, :]).then_inc(ol_ready, 1)

            split_lo(Q0 + 1)
            dve.wait_ge(sums_2, 1)
            V.tensor_scalar(small(QV, TT), bank[4][:, 0:TT], 1.0 / D, EPS, ALU.mult, ALU.add).then_inc(var_2, 1)
            dve.wait_ge(spread_2, 1)
            V.tensor_copy(rstd_q[:], bank[4][:]).then_inc(spread_2_read, 1)
            dve.wait_ge(spread_2_read, 1)
            q_lo(0)
            split_lo(Q0 + 2)
            q_lo(1)
            softmax(0)
            split_lo(Q0 + 3)
            q_lo(2)
            pt_lo(0)
            softmax(1)
            o_lo(0)
            split_lo(Q0 + 4)
            q_lo(3)
            pt_lo(1)
            softmax(2)
            o_lo(1)
            split_lo(XO0 + 1)
            pt_lo(2)
            softmax(3)
            o_lo(2)
            pt_lo(3)
            o_lo(3)
            for n in range(4):
                if n > 1:
                    split_lo(XO0 + n + 1)
                for t in range(2):
                    i = 2 * n + t
                    if i == 1:
                        split_lo(XO0 + 2)
                    dve.wait_ge(xo_even if t == 0 else panel_done, n + 1 if t == 0 else XO0 + n + 1)
                    V.tensor_tensor(X[:, i, :], bank[2 * (n % 2) + t][:], X[:, i, :], ALU.add).then_inc(x3_ready, 1)
                    residual_lo(i, C_FFN, 2 * KT)
            dve.wait_ge(sums_3, 1)
            V.tensor_scalar(small(GV, TT), bank[4][:, 0:TT], 1.0 / D, EPS, ALU.mult, ALU.add).then_inc(var_3, 1)
            split_lo(FI0 + 1)
            dve.wait_ge(spread_3, 1)
            V.tensor_copy(rstd_f[:], bank[4][:]).then_inc(spread_3_read, 1)
            dve.wait_ge(spread_3_read, 1)
            with dve.Fori(0, HT // 2) as it:
                for t in range(2):
                    dve.wait_ge(gate_even if t == 0 else panel_done, it * 1 + 1 if t == 0 else it * 2 + (FI0 + 1))
                    V.tensor_tensor(gt[:, t, :], bank[t][:], rstd_f[:], ALU.mult).then_inc(g_scaled, 1)
                dve.wait_ge(hi_ready, it * 2 + (FI0 + 3))
                lo(wl[:, 0, :], raw[:, 0, :], wh[:, 0, :]).then_inc(lo_ready, 1)
                for t in range(2):
                    dve.wait_ge(up_even if t == 0 else panel_done, it * 1 + 1 if t == 0 else it * 2 + (FI0 + 2))
                    V.tensor_tensor(ut[:, t, :], bank[2 + t][:], rstd_f[:], ALU.mult).then_inc(u_scaled, 1)
                    dve.wait_ge(u_scaled, it * 2 + (t + 1))
                    dve.wait_ge(silu_ready, it * 2 + (t + 1))
                    V.tensor_tensor(ut[:, t, :], ut[:, t, :], gt[:, t, :], ALU.mult).then_inc(u_prod, 1)
                    dve.wait_ge(hidh_ready, it * 2 + (t + 1))
                    lo(hidl[:, it * 2 + t, :], ut[:, t, :], hidh[:, it * 2 + t, :]).then_inc(hidl_ready, 1)
                dve.wait_ge(hi_ready, it * 2 + (FI0 + 4))
                lo(wl[:, 1, :], raw[:, 1, :], wh[:, 1, :]).then_inc(lo_ready, 1)
            for n in range(FO0 + 2, PANELS):
                split_lo(n)
            dve.wait_ge(gf_here, 16)
            for t in range(TT):
                dve.wait_ge(f_sq, 2 * t + 2)
                chain(V.tensor_tensor(small(FV + t), small(FS + 2 * t), small(FS + 2 * t + 1), ALU.add))
                V.tensor_scalar(small(FV + t), small(FV + t), 1.0 / D, EPS, ALU.mult, ALU.add).then_inc(f_var, 1)
                dve.wait_ge(f_rstd, t + 1)
                for half in range(2):
                    cs = slice(half * S, (half + 1) * S)
                    V.scalar_tensor_tensor(out=outb[:, t, cs], in0=bank[(4 + 2 * t + half) % 8][:], scalar=small(FR + t),
                                           in1=gf[:, cs], op0=ALU.mult, op1=ALU.mult).then_inc(f_out, 1)

        @block.tensor
        def _(pe):
            def mm3(dst, lh, ll, rh, rl, start, stop):
                nc.tensor.matmul(dst, lh, rh, start=start, stop=False)
                nc.tensor.matmul(dst, lh, rl, start=False, stop=False)
                return nc.tensor.matmul(dst, ll, rh, start=False, stop=stop)

            def fm_tile(dst, slot, t, rh, rl, ks=range(KT), first=0, ready=None, free=None):
                for k in ks:
                    if ready:
                        pe.wait_ge(ready[0], ready[1] + k + 1)
                    c = slice(k * 256 + t * P, k * 256 + (t + 1) * P)
                    ins = mm3(dst, wh[:, slot, c], wl[:, slot, c], rh(k), rl(k), k == 0, k == KT - 1)
                return ins

            def fm_panel(n, rh, rl, even, free, ready=None, width=S):
                pe.wait_ge(lo_ready, n + 1)
                for t in range(2):
                    if free:
                        pe.wait_ge(*free[t])
                    ins = fm_tile(bank[2 * (n % 2) + t][:, 0:width], n % SLOTS, t, rh, rl, ready=ready)
                    ins.then_inc(even if t == 0 else panel_done, 1)

            def tm_pair(n, banks, lhs, even, before=None, between=None):
                for half in range(2):
                    if half and between:
                        between()
                    pe.wait_ge(lo_ready, n + half + 1)
                    for t, b in enumerate(banks):
                        if half == 0 and before:
                            before(t)
                        for k in range(4):
                            c = slice(k * S, (k + 1) * S)
                            slot = (n + half) % SLOTS
                            ins = mm3(bank[b][:], *lhs(4 * half + k, t), wh[:, slot, c], wl[:, slot, c],
                                      half == 0 and k == 0, half == 1 and k == 3)
                        if t == len(banks) - 1:
                            ins.then_inc(panel_done, 1)
                        elif half == 1:
                            ins.then_inc(even, 1)

            def sum_columns(dst, acc, tiles):
                for t in range(tiles):
                    ins = nc.tensor.matmul(dst[:, t:t + 1], acc[:, t * P:(t + 1) * P], ones[:, 0:1], start=True, stop=True)
                return ins

            def spread(dst, first, tiles):
                for t in range(tiles):
                    ins = nc.tensor.matmul(dst[:, t * P:(t + 1) * P], small(first + t).to_broadcast([P, P]), ident[:],
                                           start=True, stop=True)
                return ins

            h_hi, h_lo = (lambda k: hh[:, k, :]), (lambda k: hl[:, k, :])

            for n in range(4):
                for t in range(2):
                    for ks in (range(4), range(4, 8)):
                        if ks[0] == 0:
                            pe.wait_ge(half_lo, K0 + n + 1)
                        else:
                            pe.wait_ge(lo_ready, K0 + n + 1)
                        ins = fm_tile(bank[n][:, t * M:(t + 1) * M], (K0 + n) % SLOTS, t, lambda k: memh[:, k, :],
                                      lambda k: meml[:, k, :], ks=ks, ready=(meml_ready, 0))
                ins.then_inc(panel_done, 1)
                if n == 0:
                    pe.wait_ge(acc_m_ready, 1)
                    pe.wait_ge(const_ready, 3)
                    sum_columns(bank[4], acc_m, MT).then_inc(sums_m, 1)
                if n == 1:
                    pe.wait_ge(rstd_m_ready, 1)
                    spread(bank[4][:, 0:M], RM, MT)
                    spread(bank[4][:, M:2 * M], RM, MT).then_inc(spread_m, 1)
            def mem_pair(k, t):
                return memh[:, k, t * P:(t + 1) * P], meml[:, k, t * P:(t + 1) * P]

            def sums_of_x():
                pe.wait_ge(acc_x_ready, 1)
                pe.wait_ge(kl_ready, 1)
                sum_columns(bank[0], acc_x, TT).then_inc(sums_x, 1)

            tm_pair(V0, (6, 7), mem_pair, v_even, between=sums_of_x)
            pe.wait_ge(rstd_x_ready, 1)
            pe.wait_ge(kl_ready, 4)
            spread(bank[3], XR, TT).then_inc(spread_x, 1)
            tm_pair(V0 + 2, (4, 5), mem_pair, v_even, before=lambda t: pe.wait_ge(spread_m_read, 1))

            def h_pair(k, t):
                pe.wait_ge(hl_ready, k + 1)
                return hh[:, k, t * P:(t + 1) * P], hl[:, k, t * P:(t + 1) * P]


            def sv_bank_free(t):
                if t == 0:
                    pe.wait_ge(var_x_ready, 1)
                if t == 3:
                    pe.wait_ge(xs_ready, KT)

            tm_pair(SV0, (0, 1, 2, 3), h_pair, sv_tile, before=sv_bank_free)
            tm_pair(SU0, (4, 5, 6, 7), h_pair, su_tile, before=lambda t: pe.wait_ge(vl_ready, 4))
            for n in range(2):
                fm_panel(GC0 + n, h_hi, h_lo, gc_even, [(sv_gelu, 2 * n + t + 1) for t in range(2)])
            pe.wait_ge(svl_ready, TT)
            pe.wait_ge(wsl_ready, 1)
            for g in range(4):
                pe.wait_ge(su_gelu, g + 1)
                c = slice(g * P, (g + 1) * P)
                mm3(bank[4 + g][:].rearrange("p (c d) -> p c d", c=TT), wsh[:, g, :], wsl[:, g, :],
                    svh[:, :, c], svl[:, :, c], True, True).then_inc(mixed, 1)
            for n in range(2):
                fm_panel(XI0 + n, h_hi, h_lo, xi_even, [(gc_ready, 2 * n + t + 1) for t in range(2)])
            for g in range(4):
                pe.wait_ge(a_tok, g + 1)
                for t in range(TT):
                    ins = nc.tensor.transpose(bank[4 + g][:, t * P:(t + 1) * P], ug[:, t, g * P:(g + 1) * P], ident[:])
                ins.then_inc(a_fm, 1)
            for n in range(2):
                fm_panel(PC0 + n, h_hi, h_lo, pc_even, [(cx_ready, 2 * n + t + 1) for t in range(2)])
            for n in range(2):
                fm_panel(GB0 + n, h_hi, h_lo, gb_even, [(zp_ready, 2 * n + t + 1) for t in range(2)])
            pe.wait_ge(wgl_ready, 1)
            for g in range(4):
                pe.wait_ge(pooll_ready, g + 1)
                pe.wait_ge(actl_ready, g + 1)
                mm3(bank[4 + g][:], wgh[:, g, :], wgl[:, g, :], acth[:, 2 * BT + g, :], actl[:, 2 * BT + g, :],
                    True, True).then_inc(pool_lin, 1)

            def gate_panel(b, half, j):
                slot = (3 * half + j) % 2
                pe.wait_ge(lo_ready, b * 6 + (GA0 + 3 * half + j + 1))
                for t in range(2):
                    pe.wait_ge(low_read, b * 8 + (4 * half + 2 * j + t + 1))
                    ins = fm_tile(bank[2 * j + t][:], slot, t, h_hi, h_lo)
                    ins.then_inc(ga_even if t == 0 else panel_done, 1)

            def branch_panel(b, half):
                slot = (3 * half + 2) % 2
                pe.wait_ge(lo_ready, b * 6 + (GA0 + 3 * half + 3))
                for t in range(4):
                    pe.wait_ge(high_read, b * 8 + (4 * half + t + 1))
                    if t == 0:
                        pe.wait_ge(high_read, 4)
                        pe.wait_ge(actl_ready, 2 * BT)
                    for k in range(BT):
                        c = slice(k * S + t * P, k * S + (t + 1) * P)
                        ins = mm3(bank[4 + t][:], wh[:, slot, c], wl[:, slot, c], acth[:, b * BT + k, :],
                                  actl[:, b * BT + k, :], k == 0, k == BT - 1)
                    ins.then_inc(br_tile if t < 3 else panel_done, 1)

            with pe.Fori(0, 3) as b:
                for half in range(2):
                    gate_panel(b, half, 0)
                    gate_panel(b, half, 1)
                    branch_panel(b, half)
            for n in range(4):
                fm_panel(WO0 + n, lambda k: mh[:, k, :], lambda k: ml[:, k, :], wo_even,
                         [(low_read, 4 + 20 + 2 * n + t + 1) if n < 2 else (x2_ready, 2 * (n - 2) + t + 1) for t in range(2)],
                         ready=(ml_ready, 0))

            def q_panel(h):
                n = Q0 + h
                pe.wait_ge(lo_ready, n + 1)
                for t in range(2):
                    pe.wait_ge(*((x2_ready, 2 * (h + 2) + t + 1) if h < 2 else (ql_ready, 2 * (h - 2) + t + 1)))
                    ins = fm_tile(bank[2 * (h % 2) + t][:], n % SLOTS, t, h_hi, h_lo, ready=(hl_ready, KT))
                    ins.then_inc(q_even if t == 0 else panel_done, 1)
                    if h == 0 and t == 0:
                        pe.wait_ge(acc_2, 1)
                        pe.wait_ge(high_read, 4 + 20 + 1)
                        sum_columns(bank[4], acc2, TT).then_inc(sums_2, 1)
                    if h == 0 and t == 1:
                        pe.wait_ge(rstd_2, 1)
                        spread(bank[4], QR, TT).then_inc(spread_2, 1)

            def score(h):
                pe.wait_ge(ql_ready, 2 * h + 2)
                if h == 0:
                    pe.wait_ge(spread_2_read, 1)
                    pe.wait_ge(high_read, 4 + 20 + 2)
                else:
                    pe.wait_ge(exp_ready, TT * h)
                for t in range(TT):
                    dst = bank[4 + t // 2][:, (t % 2) * M:(t % 2 + 1) * M]
                    for d in range(2):
                        c = slice(t * P, (t + 1) * P)
                        ins = mm3(dst, qh[:, h % 2, d, c], ql[:, h % 2, d, c], kh[:, 2 * h + d, :], kl[:, 2 * h + d, :],
                                  d == 0, d == 1)
                ins.then_inc(scores, 1)

            def transpose_probs(h):
                pe.wait_ge(probs, TT * (h + 1))
                if h == 0:
                    pe.wait_ge(high_read, 4 + 24)
                else:
                    pe.wait_ge(ol_ready, 2 * h)
                for mt in range(MT):
                    for t in range(TT):
                        ins = nc.tensor.transpose(bank[6 + mt][:, t * P:(t + 1) * P], pr[:, h % 2, t, mt * P:(mt + 1) * P], ident[:])
                    ins.then_inc(probs_t, 1)

            def head_out(h):
                pe.wait_ge(ptl_ready, 2 * h + 2)
                for t in range(2):
                    for mt in range(MT):
                        c = slice(h * HD + t * P, h * HD + (t + 1) * P)
                        ins = mm3(bank[6 + t][:], vh[:, mt, c], vl[:, mt, c], pth[:, h % 2, mt, :], ptl[:, h % 2, mt, :],
                                  mt == 0, mt == MT - 1)
                    ins.then_inc(heads_out, 1)

            def out_part(n, ks, done=False):
                pe.wait_ge(lo_ready, XO0 + n + 1)
                for t in range(2):
                    if ks[0] == 0:
                        pe.wait_ge(*((ql_ready, 2 * (n + 2) + t + 1) if n < 2 else (x3_ready, 2 * (n - 2) + t + 1)))
                    ins = fm_tile(bank[2 * (n % 2) + t][:], (XO0 + n) % SLOTS, t, lambda k: oh[:, k, :],
                                  lambda k: ol[:, k, :], ks=ks, ready=(ol_ready, 0))
                    if done:
                        ins.then_inc(xo_even if t == 0 else panel_done, 1)

            q_panel(0)
            q_panel(1)
            score(0)
            q_panel(2)
            transpose_probs(0)
            score(1)
            head_out(0)
            q_panel(3)
            transpose_probs(1)
            score(2)
            head_out(1)
            out_part(0, range(0, 2))
            out_part(0, range(2, 4))
            transpose_probs(2)
            score(3)
            head_out(2)
            out_part(1, range(0, 2))
            transpose_probs(3)
            out_part(0, range(4, 6))
            head_out(3)
            out_part(1, range(2, 4))
            out_part(0, range(6, 8), True)
            out_part(1, range(4, 8), True)
            out_part(2, range(8), True)
            out_part(3, range(8), True)

            def ffn_in(it, first):
                for j in range(2):
                    n = FI0 + j
                    pe.wait_ge(lo_ready, it * 2 + (n + 1))
                    for t in range(2):
                        if first:
                            pe.wait_ge(x3_ready, 4 + 2 * j + t + 1)
                        else:
                            pe.wait_ge(g_scaled if j == 0 else u_scaled, it * 2 + (t - 1))
                        ins = fm_tile(bank[2 * j + t][:], n % SLOTS, t, h_hi, h_lo, ready=(hl_ready, 2 * KT) if first else None)
                        ins.then_inc((gate_even if j == 0 else up_even) if t == 0 else panel_done, 1)
                        if first and j == 0 and t == 0:
                            pe.wait_ge(acc_3, 1)
                            pe.wait_ge(exp_ready, TT * HEADS)
                            sum_columns(bank[4], acc2, TT).then_inc(sums_3, 1)
                        if first and j == 0 and t == 1:
                            pe.wait_ge(rstd_3, 1)
                            spread(bank[4], GR, TT).then_inc(spread_3, 1)

            ffn_in(0, True)
            with pe.Fori(1, HT // 2) as it:
                ffn_in(it, False)
            for n in range(HT // 2):
                pe.wait_ge(lo_ready, FO0 + n + 1)
                pe.wait_ge(hidl_ready, 2 * n + 2)
                slot = (FO0 + n) % SLOTS
                for t in range(TT):
                    for half in range(2):
                        b = (4 + 2 * t + half) % 8
                        if n == 0:
                            if b == 4:
                                pe.wait_ge(spread_3_read, 1)
                                pe.wait_ge(ol_ready, 2 * HEADS)
                            elif b < 2:
                                pe.wait_ge(g_scaled, HT)
                            elif b < 4:
                                pe.wait_ge(u_scaled, HT)
                            for k in range(4):
                                nc.tensor.matmul(bank[b][:, k * P:(k + 1) * P], X[:, 4 * half + k, t * P:(t + 1) * P], ident[:],
                                                 is_transpose=True, start=k == 0, stop=False)
                        for k in range(2):
                            c = slice(k * D + half * S, k * D + (half + 1) * S)
                            r = slice(t * P, (t + 1) * P)
                            ins = mm3(bank[b][:], hidh[:, 2 * n + k, r], hidl[:, 2 * n + k, r], wh[:, slot, c], wl[:, slot, c],
                                      False, n == HT // 2 - 1 and k == 1)
                        if (t, half) == (TT - 1, 1):
                            ins.then_inc(panel_done, 1)
                        elif n == HT // 2 - 1:
                            ins.then_inc(fo_tile, 1)


def fm(w):
    n = w.shape[1] // 256
    return w.reshape(KT, P, n, 256).transpose(2, 1, 0, 3).reshape(n, P, PANEL)


def tm(w, width):
    k = PANEL // width
    nk, nc_ = w.shape[0] // (k * P), w.shape[1] // width
    return w.reshape(nk, k, P, nc_, width).transpose(3, 0, 2, 1, 4).reshape(nk * nc_, P, PANEL)


def columns(v):
    return v.reshape(-1, P).T


def kernel(**inputs):
    import concourse.bacc as bacc
    from concourse.bass_utils import run_bass_kernel_spmd

    a = {k: np.asarray(v) for k, v in inputs.items()}
    w_in = a["w_in"][0]
    u, v, gb, gc, xi, pc, gates = np.split(w_in, [512, 1024, 1536, 2048, 2560, 3072], axis=1)
    gates = fm(gates)
    branch = [tm(a[n][0], 512) for n in ("w_branch_a", "w_branch_b", "w_branch_c")]
    ga = []
    for b in range(3):
        for half in range(2):
            ga += [gates[4 * b + 2 * half:4 * b + 2 * half + 2], branch[b][half:half + 1]]
    w_k, w_v = np.split(a["w_xkv"][0], 2, axis=1)
    f_gate, f_up = np.split(a["w_ffn_in"][0], 2, axis=1)
    ffn = np.stack([fm(f_gate), fm(f_up)], axis=1).reshape(HT, P, PANEL)
    weights = np.concatenate([fm(w_k), tm(w_v, 512), tm(v, 512), tm(u, 512), fm(gc), fm(xi), fm(pc), fm(gb)] + ga
                             + [fm(a["w_o"][0]), fm(a["w_xq"][0]), fm(a["w_xo"][0]), ffn, tm(a["w_ffn_out"][0], 1024)])
    inv = 1.0 / np.minimum(np.arange(PAD) + 1, np.array([[2], [4], [8], [16]])).astype(np.float32)
    cols = np.concatenate([columns(a[n][0]) for n in ("g_mem", "g_mix", "g_xattn", "g_ffn", "b_gate", "c_scale", "b_conv")]
                          + [a["a_bs"][0].T, np.broadcast_to(inv.astype(np.float32).reshape(1, -1), (P, 4 * PAD))], axis=1)
    arrays = {
        "weights": weights,
        "x": a["x"][0].T.reshape(KT, P, S).transpose(1, 0, 2),
        "mem": a["mem"][0].T.reshape(KT, P, M).transpose(1, 0, 2),
        "cols": cols,
        "sgu": a["a_ws"][0].transpose(2, 0, 1),
        "wg": a["c_wg"][0].transpose(1, 0, 2),
        "ln_g": a["a_ln_g"],
        "ln_b": a["a_ln_b"],
        "gf": a["g_final"].reshape(1, D),
    }
    arrays = {k: np.ascontiguousarray(v) for k, v in arrays.items()}
    nc = bacc.Bacc("TRN2", target_bir_lowering=False, num_devices=1)
    aps = [nc.dram_tensor(k, v.shape, mybir.dt.from_np(v.dtype), kind="ExternalInput").ap() for k, v in arrays.items()]
    out = nc.dram_tensor("out", (S, D), F32, kind="ExternalOutput").ap()
    build(nc, *aps, out)
    r = run_bass_kernel_spmd(nc, [arrays], core_ids=[0])
    return r.results[0]["out"].reshape(1, S, D)
```
